# Optimizing a Trainium2 kernel written in Bass

```python
import math
import jax, jax.numpy as jnp
from jax import lax
import numpy as np

D_MODEL = 1024
BATCH = 1
SEQ = 512
DEPTH = 2

N_MIXERS = 2
N_HEADS = 16
HEAD_DIM = D_MODEL // N_HEADS
ATTN_WIDTH = N_HEADS * HEAD_DIM
Q_BLOCK = 128
CONV_WIDTH = D_MODEL
CONV_TAPS = 3
PLE_DIM = 256
N_ATTN_LAYERS = (DEPTH + 1) // 2
N_CONV_LAYERS = DEPTH // 2
ATTN_IN_COLS = 4 * ATTN_WIDTH + N_HEADS
CONV_IN_COLS = 4 * CONV_WIDTH
RMS_EPS = 1e-6

kernel_name = "fox_shortconv_interleaved_hybrid"

def rmsnorm(x, g):
    xf = x.astype(jnp.float32)
    y = xf * lax.rsqrt(jnp.mean(xf * xf, axis=-1, keepdims=True) + RMS_EPS)
    return (y * g.astype(jnp.float32)).astype(x.dtype)

def fox_attention(q, k, v, log_f):
    b, s, h, dh = q.shape
    nb = s // Q_BLOCK
    scale = 1.0 / math.sqrt(dh)
    c = jnp.cumsum(log_f, axis=1)
    c_keys = jnp.transpose(c, (0, 2, 1))
    q_blocks = jnp.transpose(q.reshape(b, nb, Q_BLOCK, h, dh), (1, 0, 2, 3, 4))
    c_blocks = jnp.transpose(c.reshape(b, nb, Q_BLOCK, h), (1, 0, 3, 2))
    starts = jnp.arange(nb, dtype=jnp.int32) * Q_BLOCK
    k_pos = jnp.arange(s, dtype=jnp.int32)

    def one_block(args):
        qi, ci, start = args
        logits = jnp.einsum('bqhd,bkhd->bhqk', qi, k).astype(jnp.float32) * scale
        logits = logits + ci[..., :, None] - c_keys[:, :, None, :]
        q_pos = start + jnp.arange(Q_BLOCK, dtype=jnp.int32)
        causal = k_pos[None, :] <= q_pos[:, None]
        logits = jnp.where(causal[None, None], logits, -jnp.inf)
        probs = jax.nn.softmax(logits, axis=-1)
        return jnp.einsum('bhqk,bkhd->bqhd', probs.astype(v.dtype), v)

    out = lax.map(one_block, (q_blocks, c_blocks, starts))
    return jnp.transpose(out, (1, 0, 2, 3, 4)).reshape(b, s, h, dh)

def fox_mixer(h, w_in, b_f, w_out):
    b, s, _ = h.shape
    proj = h @ w_in
    q = proj[..., 0 * ATTN_WIDTH:1 * ATTN_WIDTH].reshape(b, s, N_HEADS, HEAD_DIM)
    k = proj[..., 1 * ATTN_WIDTH:2 * ATTN_WIDTH].reshape(b, s, N_HEADS, HEAD_DIM)
    v = proj[..., 2 * ATTN_WIDTH:3 * ATTN_WIDTH].reshape(b, s, N_HEADS, HEAD_DIM)
    z = proj[..., 3 * ATTN_WIDTH:4 * ATTN_WIDTH]
    f_logit = proj[..., 4 * ATTN_WIDTH:].astype(jnp.float32) + b_f.astype(jnp.float32)
    log_f = jax.nn.log_sigmoid(f_logit)
    o = fox_attention(q, k, v, log_f).reshape(b, s, ATTN_WIDTH)
    return (o * jax.nn.silu(z)) @ w_out

def causal_depthwise_conv(u, w):
    s = u.shape[1]
    u_pad = jnp.pad(u, ((0, 0), (CONV_TAPS - 1, 0), (0, 0)))
    y = u_pad[:, 0:s] * w[0]
    for tap in range(1, CONV_TAPS):
        y = y + u_pad[:, tap:tap + s] * w[tap]
    return y

def conv_mixer(h, w_in, conv_w, w_out):
    proj = h @ w_in
    gate_b = proj[..., 0 * CONV_WIDTH:1 * CONV_WIDTH]
    gate_c = proj[..., 1 * CONV_WIDTH:2 * CONV_WIDTH]
    h_in = proj[..., 2 * CONV_WIDTH:3 * CONV_WIDTH]
    z = proj[..., 3 * CONV_WIDTH:4 * CONV_WIDTH]
    y = gate_b * causal_depthwise_conv(gate_c * h_in, conv_w)
    return (y * jax.nn.silu(z)) @ w_out

def setup_inputs(seed: int = 0) -> dict:
    key = jax.random.key(seed)
    ks = jax.random.split(key, 16)
    f32 = jnp.float32
    d = D_MODEL
    x = jax.random.normal(ks[0], (BATCH, SEQ, d), f32)
    p = jax.random.normal(ks[1], (DEPTH, BATCH, SEQ, PLE_DIM), f32)
    attn_w_in = jax.random.normal(ks[2], (N_ATTN_LAYERS, d, ATTN_IN_COLS), f32) * d ** -0.5
    attn_b_f = jax.random.uniform(ks[3], (N_ATTN_LAYERS, N_HEADS), f32, 1.0, 4.0)
    attn_w_out = jax.random.normal(ks[4], (N_ATTN_LAYERS, ATTN_WIDTH, d), f32) * ATTN_WIDTH ** -0.5
    conv_w_in = jax.random.normal(ks[5], (N_CONV_LAYERS, d, CONV_IN_COLS), f32) * d ** -0.5
    conv_kernel = jax.random.normal(ks[6], (N_CONV_LAYERS, CONV_TAPS, CONV_WIDTH), f32) * CONV_TAPS ** -0.5
    conv_w_out = jax.random.normal(ks[7], (N_CONV_LAYERS, CONV_WIDTH, d), f32) * CONV_WIDTH ** -0.5
    norm_pre = 1.0 + 0.05 * jax.random.normal(ks[8], (DEPTH, d), f32)
    norm_post = 1.0 + 0.05 * jax.random.normal(ks[9], (DEPTH, d), f32)
    pe_norm = 1.0 + 0.05 * jax.random.normal(ks[10], (DEPTH, d), f32)
    pe_w_gate = jax.random.normal(ks[11], (DEPTH, d, d), f32) * d ** -0.5
    pe_w_proj = jax.random.normal(ks[12], (DEPTH, PLE_DIM, d), f32) * PLE_DIM ** -0.5
    return {"x": x, "p": p,
            "attn_w_in": attn_w_in, "attn_b_f": attn_b_f, "attn_w_out": attn_w_out,
            "conv_w_in": conv_w_in, "conv_kernel": conv_kernel, "conv_w_out": conv_w_out,
            "norm_pre": norm_pre, "norm_post": norm_post,
            "pe_norm": pe_norm, "pe_w_gate": pe_w_gate, "pe_w_proj": pe_w_proj}

def reference(x, p, attn_w_in, attn_b_f, attn_w_out, conv_w_in, conv_kernel, conv_w_out,
              norm_pre, norm_post, pe_norm, pe_w_gate, pe_w_proj):
    for i in range(DEPTH):
        h = rmsnorm(x, norm_pre[i])
        j = i // N_MIXERS
        if i % N_MIXERS == 0:
            y = fox_mixer(h, attn_w_in[j], attn_b_f[j], attn_w_out[j])
        else:
            y = conv_mixer(h, conv_w_in[j], conv_kernel[j], conv_w_out[j])
        x = x + rmsnorm(y, norm_post[i])
        gate = jax.nn.sigmoid(rmsnorm(x, pe_norm[i]) @ pe_w_gate[i])
        x = x + gate * (p[i] @ pe_w_proj[i])
    return x


_drawn_inputs = setup_inputs


def setup_inputs(seed=0):
    import zlib

    import numpy as np

    out = dict(_drawn_inputs(seed))
    spreads = {}
    factors = {'pe_norm': 5.23}
    for name, (base, spread) in spreads.items():
        noise = np.random.default_rng([zlib.crc32(name.encode()), seed]).standard_normal(out[name].shape)
        drawn = base * np.exp(spread * noise) if base else spread * noise
        out[name] = __import__('jax').numpy.asarray(drawn.astype(out[name].dtype))
    for name, factor in factors.items():
        out[name] = (out[name] * factor).astype(out[name].dtype)
    return out
```

```python
from contextlib import ExitStack

import numpy as np
import concourse.bass as bass
from concourse import mybir

F32 = mybir.dt.float32
F32R = mybir.dt.float32r
ALU = mybir.AluOpType
ACT = mybir.ActivationFunctionType

P = 128
SEQ = 512
D = 1024
KT = D // P
TT = SEQ // P
HEADS = 16
DH = D // HEADS
PAIRS = HEADS // 2
PLE = 256
PLE_KT = PLE // P
TAPS = 3
EPS = 1e-6
MASKED = -1e30
RING = 4
RAW = 2
LOGIT_BUFS = 4
PT_STEP = (TT - 1) * P

STEP_F = 0
STEP_QKVZ = 1
STEP_OUT = [STEP_QKVZ + 4 * PAIRS, STEP_QKVZ + 4 * PAIRS + 7 * KT]
STEP_PLE = [s + KT for s in STEP_OUT]
STEP_GATE = [s + 2 * KT for s in STEP_OUT]
STEP_CONV = STEP_OUT[0] + 3 * KT
SLOT_F = 0
SLOT_QKVZ = 1
TAIL_SLOTS = 2 * KT + PLE_KT
SLOT_OUT = [SLOT_QKVZ + 4 * PAIRS, SLOT_QKVZ + 4 * PAIRS + TAIL_SLOTS + 4 * KT]
SLOT_PLE = [s + KT for s in SLOT_OUT]
SLOT_GATE = [s + KT + PLE_KT for s in SLOT_OUT]
SLOT_CONV = SLOT_OUT[0] + TAIL_SLOTS
SLOTS = SLOT_OUT[1] + TAIL_SLOTS
USE_V = 0
USE_T = -8
ACT_H = [0, 3 * KT]
ACT_U = [KT, 4 * KT]
ACT_G = [2 * KT, 5 * KT]
SCORE_AT = {0: 0, 1: 1, 2: 2, 3: 3, 5: 4, 6: 5, 7: 6, 8: 7}
TRANSPOSE_AT = {3: 0, 4: 1, 5: 2, 6: 3, 9: 4, 10: 5, 11: 6, 12: 7}
PV_AT = {8: 0, 14: 1}
GROUPS = 16


def wait(eng, sem, count):
    if not isinstance(count, int) or count > 0:
        eng.wait_ge(sem, count)


def trunk(nc, x, xT_in, pT_in, weights, b_f_in, pre_in, post_in, pe_in, taps_in, outT):
    negc_dram = nc.dram_tensor("negc_scratch", [HEADS, SEQ], F32).ap()

    ctx = ExitStack()
    with ctx:
        def sb(name, shape, dt=F32, at=ctx):
            return at.enter_context(nc.sbuf_tensor(name, shape, dt))

        def sem(name):
            return ctx.enter_context(nc.semaphore(name))

        xT = sb("xT", [P, KT, SEQ])
        act_hi = [sb(f"act{i}_hi", [P, KT, SEQ], F32R) for i in range(2)]
        act_lo = [sb(f"act{i}_lo", [P, KT, SEQ], F32R) for i in range(2)]
        w_raw = [sb(f"w_raw{i}", [P, KT, P]) for i in range(RAW)]
        w_hi = [sb(f"w_hi{i}", [P, KT, P], F32R) for i in range(RING)]
        w_lo = [sb(f"w_lo{i}", [P, KT, P], F32R) for i in range(RING)]
        ident = sb("ident", [P, P])
        future = sb("future", [P, P])
        mean_f = sb("mean_f", [P, P])
        mean_w = sb("mean_w", [P, P], F32R)
        g_pre = sb("g_pre", [P, 2, KT])
        g_post = sb("g_post", [P, 2, KT])
        g_pe = sb("g_pe", [P, 2, KT])
        taps = sb("taps", [P, TAPS, KT])
        ss = sb("ss", [P, TT])
        rms = sb("rms", [P, TT])
        rinv = sb("rinv", [P, TT])
        b_f = sb("b_f", [HEADS, 1])
        gap = sb("gap", [P, LOGIT_BUFS])
        nmax = sb("nmax", [P, LOGIT_BUFS])
        rsum = sb("rsum", [P, LOGIT_BUFS])
        rrec = sb("rrec", [P, LOGIT_BUFS])
        start = ExitStack()
        x_in = sb("x_in", [P, TT, D], at=start)
        f_part = ExitStack()
        ones_f = sb("ones_f", [HEADS, SEQ], at=f_part)
        f_x = sb("f_x", [HEADS, SEQ], at=f_part)
        f_abs = sb("f_abs", [HEADS, SEQ], at=f_part)
        f_ln = sb("f_ln", [HEADS, SEQ], at=f_part)
        f_negc = sb("f_negc", [HEADS, SEQ], at=f_part)
        f_part.close()
        x_n = sb("x_n", [P, TT, D], at=start)
        start.close()
        attn = ExitStack()
        logit = [sb(f"logit{i}", [P, SEQ], at=attn) for i in range(LOGIT_BUFS)]
        pt_hi = sb("pt_hi", [P, TT * PT_STEP + PT_STEP], F32R, attn)
        pt_lo = sb("pt_lo", [P, TT * PT_STEP + PT_STEP], F32R, attn)
        o_half = sb("o_half", [P, SEQ], at=attn)
        o_u = sb("o_u", [P, SEQ], at=attn)
        v_st = sb("v_st", [P, TT, 4 * DH], F32R, attn)
        vT = sb("vT", [P, SEQ], at=attn)
        z_tanh = sb("z_tanh", [P, SEQ], at=attn)
        z_silu = sb("z_silu", [P, SEQ], at=attn)
        q_hi = [[sb(f"q_hi{b}{h}", [P, SEQ], F32R, attn) for h in range(2)] for b in range(2)]
        q_lo = [[sb(f"q_lo{b}{h}", [P, SEQ], F32R, attn) for h in range(2)] for b in range(2)]
        k_st = [[sb(f"k_st{b}{h}", [P, SEQ], F32R, attn) for h in range(2)] for b in range(2)]
        bias = [sb(f"bias{h}", [P, TT, SEQ], at=attn) for h in range(2)]
        attn.close()
        late = ExitStack()
        conv = ExitStack()
        cv_c = sb("cv_c", [P, SEQ], at=conv)
        cv_w = sb("cv_w", [P, TAPS - 1 + SEQ], at=conv)
        cv_y = [sb(f"cv_y{i}", [P, SEQ], at=conv) for i in range(2)]
        cv_z = sb("cv_z", [P, SEQ], at=conv)
        cv_t = sb("cv_t", [P, SEQ], at=conv)
        conv.close()
        yT = sb("yT", [P, KT, SEQ], at=late)
        pleT = sb("pleT", [P, KT, SEQ], at=late)
        p_in = sb("p_in", [P, PLE_KT, SEQ], at=late)
        p_hi = sb("p_hi", [P, PLE_KT, SEQ], F32R, late)
        p_lo = sb("p_lo", [P, PLE_KT, SEQ], F32R, late)
        sq = [sb(f"sq{i}", [P, SEQ], at=late) for i in range(2)]
        acc = sb("acc", [P, SEQ], at=late)
        acc_hi = sb("acc_hi", [P, SEQ], F32R, late)
        acc_lo = sb("acc_lo", [P, SEQ], F32R, late)
        rs_root = sb("rs_root", [P, SEQ], at=late)
        rs = sb("rs", [P, SEQ], at=late)
        rs2 = sb("rs2", [P, SEQ], at=late)
        t_a = [sb(f"t_a{i}", [P, SEQ], at=late) for i in range(2)]
        t_b = [sb(f"t_b{i}", [P, SEQ], at=late) for i in range(2)]
        late.close()

        ps_pj = [ctx.enter_context(nc.psum_tensor(f"ps_pj{i}", [P, SEQ], F32)) for i in range(2)]
        ps_sc = [ctx.enter_context(nc.psum_tensor(f"ps_sc{i}", [P, SEQ], F32)) for i in range(2)]
        ps_tr = [ctx.enter_context(nc.psum_tensor(f"ps_tr{i}", [P, SEQ], F32)) for i in range(2)]
        ps_o = [ctx.enter_context(nc.psum_tensor(f"ps_o{i}", [P, SEQ], F32)) for i in range(2)]

        x_loaded = [sem(f"x_loaded{t}") for t in range(TT)]
        g_loaded = [sem(f"g_loaded{i}") for i in range(5)]
        p_loaded = sem("p_loaded")
        w_loaded = [sem(f"w_loaded{i}") for i in range(RAW)]
        res_loaded = sem("res_loaded")
        w_hi_done = sem("w_hi_done")
        w_ready = sem("w_ready")
        pj_done = sem("pj_done")
        pj_free = [sem(f"pj_free{i}") for i in range(2)]
        xn_done = sem("xn_done")
        tr_done = sem("tr_done")
        tr_free = [sem(f"tr_free{i}") for i in range(2)]
        consts = sem("consts")
        mean_ready = sem("mean_ready")
        x_ss = sem("x_ss")
        x_root = sem("x_root")
        x_rinv = sem("x_rinv")
        x_norm = sem("x_norm")
        act_hi_done = sem("act_hi_done")
        act_ready = sem("act_ready")
        f_chain = sem("f_chain")
        f_act = sem("f_act")
        negc_stored = sem("negc_stored")
        bias_loaded = [sem(f"bias_loaded{h}") for h in range(2)]
        bias_ready = [sem(f"bias_ready{h}") for h in range(2)]
        q_hi_done = sem("q_hi_done")
        k_hi_done = sem("k_hi_done")
        v_hi_done = sem("v_hi_done")
        z_tanh_done = sem("z_tanh_done")
        sc_done = sem("sc_done")
        logit_ready = sem("logit_ready")
        exp_done = sem("exp_done")
        rec_done = sem("rec_done")
        prob_ready = sem("prob_ready")
        pt_hi_done = sem("pt_hi_done")
        pv_done = sem("pv_done")
        o_half_done = sem("o_half_done")
        o_free = sem("o_free")
        u_ready = sem("u_ready")
        p_hi_done = sem("p_hi_done")
        p_ready = sem("p_ready")
        sq_ready = sem("sq_ready")
        acc_done = sem("acc_done")
        acc_hi_done = sem("acc_hi_done")
        acc_ready = sem("acc_ready")
        st_done = sem("st_done")
        root_done = sem("root_done")
        rs_ready = sem("rs_ready")
        x_new = sem("x_new")
        v_self = sem("v_self")
        g_tanh = sem("g_tanh")
        cv_pad = sem("cv_pad")
        cv_self = sem("cv_self")
        cz_tanh = sem("cz_tanh")
        stored = sem("stored")

        block = ctx.enter_context(nc.Block())

        def count(c, per, m0, jj):
            return c + per * m0 + 2 * per * jj

        def halved(c, per, m0, jj):
            return (c + per * m0) // 2 + per * jj

        def last_step(slot):
            for l in range(2):
                if SLOT_PLE[l] <= slot < SLOT_GATE[l]:
                    return STEP_GATE[l] - 1
            passed = sum(slot >= SLOT_GATE[l] for l in range(2))
            return slot + passed * (KT - PLE_KT)

        def causal(pt, i):
            part = pt[:, i * P:i * P + PT_STEP * (i + 1)]
            return part.rearrange("p (k c) -> p k c", c=PT_STEP)[:, :, 0:P]

        @block.sync
        def _(sp):
            def load_slot(slot, place):
                wait(sp, w_ready, slot - RAW + 1)
                src = weights[bass.ds(slot, 1), :, :].rearrange("o p (k c) -> p (o k) c", c=P)
                sp.dma_start(w_raw[place % RAW][:], src).then_inc(w_loaded[place % RAW], 16)

            def load_bias(a, h):
                wait(sp, logit_ready, 8 * a - 8 + 4 * h + 4)
                for i in range(TT):
                    n = (i + 1) * P
                    row = negc_dram[bass.ds(2 * a + h, 1), 0:n]
                    sp.dma_start(bias[h][:, i, 0:n], row.to_broadcast([P, n])).then_inc(bias_loaded[h], 16)

            for t in range(TT):
                sp.dma_start(x_in[:, t, :], x[t * P:(t + 1) * P, :]).then_inc(x_loaded[t], 16)
                if t == 1:
                    load_slot(0, 0)
            sp.dma_start(g_pre[:], pre_in).then_inc(g_loaded[0], 16)
            sp.dma_start(b_f[:], b_f_in).then_inc(g_loaded[1], 16)
            for slot in range(1, 6):
                load_slot(slot, slot)
            sp.dma_start(g_post[:], post_in).then_inc(g_loaded[2], 16)
            sp.dma_start(g_pe[:], pe_in).then_inc(g_loaded[3], 16)
            sp.dma_start(taps[:], taps_in).then_inc(g_loaded[4], 16)
            sp.wait_ge(f_chain, 3)
            sp.dma_start(negc_dram, f_negc[:]).then_inc(negc_stored, 16)
            sp.wait_ge(negc_stored, 16)

            def turn(m):
                load_slot(6 + 4 * m, 6)
                load_bias(m, 0)
                load_slot(7 + 4 * m, 7)
                load_slot(8 + 4 * m, 8)
                load_bias(m, 1)
                load_slot(9 + 4 * m, 9)

            turn(0)
            sp.dma_start(xT[:], xT_in.rearrange("k p t -> p k t")).then_inc(res_loaded, 16)
            with sp.Fori(1, PAIRS) as m:
                turn(m)
            for slot in range(6 + 4 * PAIRS, SLOT_CONV + RAW):
                load_slot(slot, slot)
                if slot == 7 + 4 * PAIRS:
                    sp.wait_ge(act_ready, ACT_U[0] + KT)
                    sp.dma_start(p_in[:], pT_in[0]).then_inc(p_loaded, 16)
            with sp.Fori(0, KT) as m:
                for j in range(4):
                    load_slot(4 * m + SLOT_CONV + RAW + j, SLOT_CONV + RAW + j)
            sp.wait_ge(p_ready, 1)
            sp.dma_start(p_in[:], pT_in[1]).then_inc(p_loaded, 16)
            for slot in range(SLOT_OUT[1] + RAW, SLOTS):
                load_slot(slot, slot)
            for m in range(KT):
                sp.wait_ge(x_new, 3 * KT + m + 1)
                sp.dma_start(outT[m], xT[:, m, :]).then_inc(stored, 16)
            sp.wait_ge(stored, 16 * KT)

        @block.gpsimd
        def _(pool):
            nc.gpsimd.memset(ident[:], 0.0).then_inc(consts, 1)
            pool.wait_ge(consts, 1)
            nc.gpsimd.affine_select(out=ident[:], in_=ident[:], compare_op=ALU.not_equal, fill=1.0, base=0,
                                    pattern=[[-1, P]], channel_multiplier=1).then_inc(consts, 1)
            nc.gpsimd.memset(mean_f[:], 1.0 / D).then_inc(consts, 1)
            nc.gpsimd.memset(future[:], 0.0).then_inc(consts, 1)
            pool.wait_ge(consts, 4)
            nc.gpsimd.affine_select(out=future[:], in_=future[:], compare_op=ALU.is_ge, fill=MASKED, base=0,
                                    pattern=[[-1, P]], channel_multiplier=1).then_inc(consts, 1)
            pool.wait_ge(consts, 5)

            def weight_lo(slot, place):
                pool.wait_ge(w_hi_done, slot + 1)
                nc.gpsimd.tensor_tensor(w_lo[place % RING][:], w_raw[place % RAW][:], w_hi[place % RING][:],
                                        ALU.subtract).then_inc(w_ready, 1)

            def mask(a, h):
                pool.wait_ge(bias_loaded[h], 64 * a + 64)
                for i in range(TT):
                    diagonal = bias[h][:, i, i * P:(i + 1) * P]
                    nc.gpsimd.tensor_tensor(diagonal, diagonal, future[:], ALU.add).then_inc(bias_ready[h], 1)

            def turn(m):
                weight_lo(4 + 4 * m, 4)
                weight_lo(5 + 4 * m, 5)
                mask(m, 0)
                weight_lo(6 + 4 * m, 6)
                weight_lo(7 + 4 * m, 7)
                mask(m, 1)

            for slot in range(4):
                weight_lo(slot, slot)
            with pool.Fori(0, PAIRS) as m:
                turn(m)

            def add_square(n):
                pool.wait_ge(sq_ready, n + 1)
                if n % KT == 0:
                    wait(pool, acc_ready, n // KT)
                    nc.gpsimd.tensor_copy(acc[:], sq[n % 2][:]).then_inc(acc_done, 1)
                else:
                    pool.wait_ge(acc_done, n)
                    nc.gpsimd.tensor_tensor(acc[:], acc[:], sq[n % 2][:], ALU.add).then_inc(acc_done, 1)

            for l in range(2):
                for m in range(KT):
                    weight_lo(SLOT_OUT[l] + m + 3, SLOT_OUT[l] + m + 3)
                    add_square(3 * KT * l + m)
                weight_lo(SLOT_GATE[l] + 1, SLOT_GATE[l] + 1)
                for m in range(KT):
                    add_square(3 * KT * l + KT + m)
                weight_lo(SLOT_GATE[l] + 2, SLOT_GATE[l] + 2)
                for m in range(KT):
                    if SLOT_GATE[l] + m + 3 < SLOTS:
                        weight_lo(SLOT_GATE[l] + m + 3, SLOT_GATE[l] + m + 3)
                    if l == 0:
                        add_square(2 * KT + m)
                if l == 0:
                    with pool.Fori(0, KT) as m:
                        for j in range(4):
                            weight_lo(4 * m + SLOT_CONV + 3 + j, SLOT_CONV + 3 + j)

        @block.scalar
        def _(act):
            def weight_hi(slot, place):
                act.wait_ge(w_loaded[place % RAW], 16 * (place // RAW + 1) + (16 // RAW) * (slot - place))
                if place >= RING:
                    act.wait_ge(pj_done, last_step(place - RING) + 1 + (slot - place))
                nc.scalar.copy(w_hi[place % RING][:], w_raw[place % RAW][:]).then_inc(w_hi_done, 1)

            for t in range(TT):
                act.wait_ge(x_loaded[t], 16)
                nc.scalar.activation(x_n[:, t, :], x_in[:, t, :], ACT.Square, accum_out=ss[:, t:t + 1]).then_inc(x_ss, 1)
                act.wait_ge(x_ss, t + 1)
                nc.scalar.activation(rms[:, t:t + 1], ss[:, t:t + 1], ACT.Sqrt, scale=1.0 / D,
                                     bias=EPS).then_inc(x_root, 1)
            act.wait_ge(g_loaded[0], 16)
            weight_hi(0, 0)
            for k in range(KT):
                act.wait_ge(xn_done, k + 1)
                nc.scalar.activation(act_hi[0][:, k, :], ps_tr[k % 2][:], ACT.Copy,
                                     scale=g_pre[:, 0, k:k + 1]).then_inc(act_hi_done, 1)
                if k % 2 == 1 and k < 6:
                    weight_hi((k + 1) // 2, (k + 1) // 2)

            def score_exp(u, m0, jj):
                act.wait_ge(logit_ready, count(u + 1 - 8, 8, m0, jj))
                b, n = u % LOGIT_BUFS, (u % TT + 1) * P
                nc.scalar.activation(logit[b][:, 0:n], logit[b][:, 0:n], ACT.Exp, scale=-1.0, bias=nmax[:, b:b + 1],
                                     accum_out=rsum[:, b:b + 1]).then_inc(exp_done, 1)

            def pt_round(u, m0, jj):
                n = USE_T + 9 * m0 + u
                act.wait_ge(tr_done, count(USE_T + u + 1, 9, m0, jj))
                if u % TT == 0:
                    wait(act, pv_done, count(u // TT - 2, 2, m0, jj))
                i = u % TT
                nc.scalar.copy(causal(pt_hi, i), ps_tr[n % 2][:, 0:(i + 1) * P].rearrange("p (k c) -> p k c", c=P)
                               ).then_inc(pt_hi_done, 1)

            def head_half(h, m0, jj):
                act.wait_ge(pv_done, count(h - 1, 2, m0, jj))
                wait(act, o_free, count(h + 1 - 4, 2, m0, jj))
                own, other = slice(h * DH, h * DH + DH), slice(DH - h * DH, 2 * DH - h * DH)
                nc.scalar.copy(o_half[own, :], ps_o[h][other, :]).then_inc(o_half_done, 1)

            def turn(m0, jj, project, attend):
                m = m0 + 2 * jj
                b = m0 % 2
                s = STEP_QKVZ + 4 * m0
                for g in range(GROUPS):
                    if g == 0 and attend:
                        act.wait_ge(pj_done, count(STEP_QKVZ, 4, m0, jj))
                        nc.scalar.activation(z_tanh[:], ps_pj[(s - 1) % 2][:], ACT.Tanh, scale=0.5
                                             ).then_inc(z_tanh_done, 1)
                    if g == 4 and project:
                        act.wait_ge(pj_done, count(STEP_QKVZ + 1, 4, m0, jj))
                        for h in range(2):
                            for r in range(2):
                                last = nc.scalar.mul(q_hi[b][h][r * DH:r * DH + DH, :],
                                                     ps_pj[s % 2][h * DH:h * DH + DH, :], DH ** -0.5)
                        last.then_inc(q_hi_done, 1)
                    if g == 8 and project:
                        act.wait_ge(pj_done, count(STEP_QKVZ + 2, 4, m0, jj))
                        for h in range(2):
                            own = slice(h * DH, h * DH + DH)
                            last = nc.scalar.copy(k_st[b][h][own, :], ps_pj[(s + 1) % 2][own, :])
                        last.then_inc(k_hi_done, 1)
                    if g == 12 and project:
                        act.wait_ge(pj_done, count(STEP_QKVZ + 3, 4, m0, jj))
                        nc.scalar.copy(vT[:], ps_pj[(s + 2) % 2][:]).then_inc(pj_free[(s + 2) % 2], 1)
                    if attend and g in SCORE_AT:
                        score_exp(SCORE_AT[g], m0, jj)
                    if attend and g in TRANSPOSE_AT:
                        pt_round(TRANSPOSE_AT[g], m0, jj)
                    if g % 4 == 1 and project:
                        weight_hi(count(4 + g // 4, 4, m0, jj), 4 + 4 * m0 + g // 4)
                    if not attend and g == 0:
                        act.wait_ge(f_chain, 1)
                        nc.scalar.activation(f_ln[:], f_abs[:], ACT.Exp, scale=-1.0).then_inc(f_act, 1)
                        act.wait_ge(f_act, 1)
                        nc.scalar.activation(f_ln[:], f_ln[:], ACT.Ln, bias=1.0).then_inc(f_act, 1)
                    if attend and g == 9:
                        head_half(0, m0, jj)
                    if attend and g == 15:
                        head_half(1, m0, jj)
                    if g == 15 and project:
                        n = USE_V + 9 * m0
                        act.wait_ge(tr_done, count(USE_V + 1, 9, m0, jj))
                        dst = v_st[:].rearrange("p t (a b c) -> p t a b c", a=2, c=DH)
                        src = ps_tr[n % 2][:].rearrange("p (t h c) -> p t h c", h=2, c=DH)
                        for h in range(2):
                            last = nc.scalar.copy(dst[:, :, h, h, :], src[:, :, h, :])
                        last.then_inc(v_hi_done, 1)
                    if attend and g == 15:
                        act.wait_ge(u_ready, m)
                        nc.scalar.copy(act_hi[1][:, bass.ds(m - 1, 1), :], o_u[:].rearrange("p (o c) -> p o c", o=1)
                                       ).then_inc(act_hi_done, 1)

            turn(0, 0, True, False)
            turn(1, 0, True, True)
            with act.Fori(0, (PAIRS - 2) // 2) as jj:
                turn(2, jj, True, True)
                turn(3, jj, True, True)
            turn(PAIRS, 0, False, True)

            def square(n, src):
                wait(act, acc_done, n - 1)
                nc.scalar.activation(sq[n % 2][:], src, ACT.Square).then_inc(sq_ready, 1)

            def norm(n):
                act.wait_ge(acc_done, KT * (n + 1))
                wait(act, st_done, n)
                nc.scalar.copy(acc_hi[:], acc[:]).then_inc(acc_hi_done, 1)
                act.wait_ge(st_done, n + 1)
                wait(act, rs_ready, n)
                nc.scalar.activation(rs_root[:], ps_o[0][:], ACT.Sqrt, bias=EPS).then_inc(root_done, 1)

            for l in range(2):
                a_g, a_h = act_hi[l], act_hi[1 - l]
                for m in range(KT):
                    weight_hi(SLOT_OUT[l] + m + 3, SLOT_OUT[l] + m + 3)
                    s = STEP_OUT[l] + m
                    act.wait_ge(pj_done, s + 1)
                    square(3 * KT * l + m, ps_pj[s % 2][:])
                    if m == 0:
                        act.wait_ge(g_loaded[2], 16)
                    nc.scalar.activation(yT[:, m, :], ps_pj[s % 2][:], ACT.Copy, scale=g_post[:, l, m:m + 1]
                                         ).then_inc(pj_free[s % 2], 1)
                    if m == 6:
                        act.wait_ge(p_loaded, 16 * l + 16)
                        nc.scalar.copy(p_hi[:], p_in[:]).then_inc(p_hi_done, 1)
                norm(3 * l)
                weight_hi(SLOT_GATE[l] + 1, SLOT_GATE[l] + 1)
                act.wait_ge(g_loaded[3], 16)
                for m in range(KT):
                    s = STEP_PLE[l] + m
                    act.wait_ge(pj_done, s + 1)
                    nc.scalar.copy(pleT[:, m, :], ps_pj[s % 2][:]).then_inc(pj_free[s % 2], 1)
                    act.wait_ge(x_new, 2 * KT * l + m + 1)
                    nc.scalar.activation(a_g[:, m, :], xT[:, m, :], ACT.Copy, scale=g_pe[:, l, m:m + 1]
                                         ).then_inc(act_hi_done, 1)
                    square(3 * KT * l + KT + m, xT[:, m, :])
                weight_hi(SLOT_GATE[l] + 2, SLOT_GATE[l] + 2)
                norm(3 * l + 1)
                for m in range(KT):
                    if SLOT_GATE[l] + m + 3 < SLOTS:
                        weight_hi(SLOT_GATE[l] + m + 3, SLOT_GATE[l] + m + 3)
                    s = STEP_GATE[l] + m
                    act.wait_ge(pj_free[s % 2], s // 2 + 1)
                    nc.scalar.activation(t_b[m % 2][:], t_a[m % 2][:], ACT.Tanh, scale=0.5).then_inc(g_tanh, 1)
                    if l == 0:
                        act.wait_ge(x_new, KT + m + 1)
                        nc.scalar.activation(a_h[:, m, :], xT[:, m, :], ACT.Copy, scale=g_pre[:, 1, m:m + 1]
                                             ).then_inc(act_hi_done, 1)
                        square(2 * KT + m, xT[:, m, :])
                if l == 0:
                    norm(2)
                    with act.Fori(0, KT) as m:
                        for j in range(4):
                            slot = SLOT_CONV + 3 + j
                            weight_hi(4 * m + slot, slot)
                        sz = STEP_CONV + 3
                        act.wait_ge(pj_free[sz % 2], sz // 2 + 1 + 2 * m)
                        nc.scalar.activation(cv_t[:], cv_z[:], ACT.Tanh, scale=0.5).then_inc(cz_tanh, 1)
                        act.wait_ge(cv_self, 6 * m + 6)
                        nc.scalar.copy(act_hi[0][:, bass.ds(m, 1), :], cv_z[:].rearrange("p (o c) -> p o c", o=1)
                                       ).then_inc(act_hi_done, 1)

        @block.vector
        def _(dve):
            for t in range(TT):
                dve.wait_ge(x_root, t + 1)
                nc.vector.reciprocal(rinv[:, t:t + 1], rms[:, t:t + 1]).then_inc(x_rinv, 1)
                dve.wait_ge(x_rinv, t + 1)
                nc.vector.tensor_scalar(x_n[:, t, :], x_in[:, t, :], rinv[:, t:t + 1], None, ALU.mult
                                        ).then_inc(x_norm, 1)
            dve.wait_ge(g_loaded[0], 16)
            for k in range(KT):
                dve.wait_ge(act_hi_done, k + 1)
                nc.vector.scalar_tensor_tensor(act_lo[0][:, k, :], ps_tr[k % 2][:], g_pre[:, 0, k:k + 1],
                                               act_hi[0][:, k, :], ALU.mult, ALU.subtract
                                               ).then_inc(act_ready, 1)
            dve.wait_ge(consts, 3)
            nc.vector.tensor_copy(mean_w[:], mean_f[:]).then_inc(mean_ready, 1)
            nc.vector.memset(ones_f[:], 1.0).then_inc(mean_ready, 1)
            dve.wait_ge(g_loaded[1], 16)
            dve.wait_ge(pj_done, STEP_F + 1)
            nc.vector.tensor_scalar(f_x[:], ps_pj[0][0:HEADS, :], b_f[:], None, ALU.add).then_inc(pj_free[0], 1)
            dve.wait_ge(pj_free[0], 1)
            nc.vector.scalar_tensor_tensor(f_abs[:], f_x[:], -1.0, f_x[:], ALU.mult, ALU.max).then_inc(f_chain, 1)
            dve.wait_ge(f_act, 2)
            nc.vector.scalar_tensor_tensor(f_x[:], f_x[:], 0.0, f_ln[:], ALU.min, ALU.subtract).then_inc(f_chain, 1)
            dve.wait_ge(mean_ready, 2)
            dve.wait_ge(f_chain, 2)
            nc.vector.tensor_tensor_scan(f_negc[:], ones_f[:], f_x[:], 0.0, ALU.mult, ALU.subtract
                                         ).then_inc(f_chain, 1)

            def score_logits(u, m0, jj):
                h, i, b, n = u // TT, u % TT, u % LOGIT_BUFS, (u % TT + 1) * P
                dve.wait_ge(sc_done, count(u + 1 - 8, 8, m0, jj))
                if i == 0:
                    dve.wait_ge(bias_ready[h], count(0, 4, m0, jj))
                if u >= LOGIT_BUFS:
                    dve.wait_ge(tr_done, count(USE_T + u - 4 + 1, 9, m0, jj))
                else:
                    wait(dve, tr_done, count(USE_T - 9 + u + 4 + 1, 9, m0, jj))
                nc.vector.memset(gap[:, b:b + 1], 0.0)
                nc.vector.tensor_tensor_reduce(out=logit[b][:, 0:n], in0=ps_sc[u % 2][:, 0:n], in1=bias[h][:, i, 0:n],
                                               scale=-1.0, scalar=3e38, op0=ALU.add, op1=ALU.min,
                                               accum_out=nmax[:, b:b + 1]).then_inc(logit_ready, 1)

            def normalise(u, m0, jj):
                b, n = u % LOGIT_BUFS, (u % TT + 1) * P
                dve.wait_ge(exp_done, count(u + 1 - 8, 8, m0, jj))
                nc.vector.reciprocal(rrec[:, b:b + 1], rsum[:, b:b + 1]).then_inc(rec_done, 1)
                dve.wait_ge(rec_done, count(u + 1 - 8, 8, m0, jj))
                nc.vector.tensor_scalar(logit[b][:, 0:n], logit[b][:, 0:n], rrec[:, b:b + 1], None, ALU.mult
                                        ).then_inc(prob_ready, 1)

            def pt_rest(u, m0, jj):
                n, i = USE_T + 9 * m0 + u, u % TT
                dve.wait_ge(pt_hi_done, count(u + 1 - 8, 8, m0, jj))
                nc.vector.tensor_tensor(causal(pt_lo, i), ps_tr[n % 2][:, 0:(i + 1) * P].rearrange("p (k c) -> p k c", c=P),
                                        causal(pt_hi, i), ALU.subtract).then_inc(tr_free[n % 2], 1)

            def head_sum(h, m0, jj):
                dve.wait_ge(o_half_done, count(h - 1, 2, m0, jj))
                own = slice(h * DH, h * DH + DH)
                nc.vector.tensor_tensor(o_u[own, :], ps_o[h][own, :], o_half[own, :], ALU.add).then_inc(o_free, 1)

            def turn(m0, jj, project, attend):
                m = m0 + 2 * jj
                b = m0 % 2
                s = STEP_QKVZ + 4 * m0
                for g in range(GROUPS):
                    if g == 0 and attend:
                        dve.wait_ge(z_tanh_done, m)
                        nc.vector.scalar_tensor_tensor(z_silu[:], z_tanh[:], 1.0, ps_pj[(s - 1) % 2][:], ALU.add,
                                                       ALU.mult).then_inc(pj_free[(s - 1) % 2], 1)
                    if g == 4 and project:
                        dve.wait_ge(q_hi_done, m + 1)
                        for h in range(2):
                            for r in range(2):
                                part = slice(h * DH, h * DH + DH)
                                last = nc.vector.scalar_tensor_tensor(
                                    q_lo[b][h][r * DH:r * DH + DH, :], ps_pj[s % 2][part, :], DH ** -0.5,
                                    q_hi[b][h][part, :], ALU.mult, ALU.subtract)
                        last.then_inc(pj_free[s % 2], 1)
                    if g == 8 and project:
                        dve.wait_ge(k_hi_done, m + 1)
                        for h in range(2):
                            own, other = slice(h * DH, h * DH + DH), slice(DH - h * DH, 2 * DH - h * DH)
                            last = nc.vector.tensor_tensor(k_st[b][h][other, :], ps_pj[(s + 1) % 2][own, :],
                                                           k_st[b][h][own, :], ALU.subtract)
                        last.then_inc(pj_free[(s + 1) % 2], 1)
                    if attend and g - 1 in SCORE_AT:
                        normalise(SCORE_AT[g - 1], m0, jj)
                    if attend and g in SCORE_AT:
                        score_logits(SCORE_AT[g], m0, jj)
                    if attend and g in TRANSPOSE_AT:
                        pt_rest(TRANSPOSE_AT[g], m0, jj)
                    if attend and g == 9:
                        head_sum(0, m0, jj)
                    if attend and g == 15:
                        head_sum(1, m0, jj)
                    if g == 15 and project:
                        n = USE_V + 9 * m0
                        dve.wait_ge(v_hi_done, m + 1)
                        dst = v_st[:].rearrange("p t (a b c) -> p t a b c", a=2, c=DH)
                        src = ps_tr[n % 2][:].rearrange("p (t h c) -> p t h c", h=2, c=DH)
                        for h in range(2):
                            last = nc.vector.tensor_tensor(dst[:, :, h, 1 - h, :], src[:, :, h, :],
                                                           dst[:, :, h, h, :], ALU.subtract)
                        last.then_inc(tr_free[n % 2], 1)
                    if attend and g == 15:
                        dve.wait_ge(o_free, count(0, 2, m0, jj))
                        nc.vector.scalar_tensor_tensor(o_u[:], o_u[:], 0.5, z_silu[:], ALU.mult, ALU.mult
                                                       ).then_inc(u_ready, 1)
                        dve.wait_ge(act_hi_done, m + KT)
                        tile = bass.ds(m - 1, 1)
                        nc.vector.tensor_tensor(act_lo[1][:, tile, :], o_u[:].rearrange("p (o c) -> p o c", o=1),
                                                act_hi[1][:, tile, :], ALU.subtract).then_inc(act_ready, 1)

            turn(0, 0, True, False)
            turn(1, 0, True, True)
            with dve.Fori(0, (PAIRS - 2) // 2) as jj:
                turn(2, jj, True, True)
                turn(3, jj, True, True)
            turn(PAIRS, 0, False, True)

            chained = [0]

            def chain(ins):
                ins.then_inc(v_self, 1)
                chained[0] += 1
                return chained[0]

            def norm(n):
                dve.wait_ge(acc_hi_done, n + 1)
                nc.vector.tensor_tensor(acc_lo[:], acc[:], acc_hi[:], ALU.subtract).then_inc(acc_ready, 1)
                dve.wait_ge(root_done, n + 1)
                nc.vector.reciprocal(rs[:], rs_root[:]).then_inc(rs_ready, 1)
                dve.wait_ge(rs_ready, n + 1)

            for l in range(2):
                a_g, a_h = (act_hi[l], act_lo[l]), (act_hi[1 - l], act_lo[1 - l])
                dve.wait_ge(p_hi_done, l + 1)
                nc.vector.tensor_tensor(p_lo[:], p_in[:], p_hi[:], ALU.subtract).then_inc(p_ready, 1)
                norm(3 * l)
                if l == 0:
                    dve.wait_ge(res_loaded, 16)
                for m in range(KT + 1):
                    if m < KT:
                        link = chain(nc.vector.tensor_tensor(t_a[m % 2][:], yT[:, m, :], rs[:], ALU.mult))
                    if m > 0:
                        dve.wait_ge(v_self, before)
                        nc.vector.tensor_tensor(xT[:, m - 1, :], xT[:, m - 1, :], t_a[(m - 1) % 2][:], ALU.add
                                                ).then_inc(x_new, 1)
                        dve.wait_ge(act_hi_done, ACT_G[l] + m)
                        nc.vector.scalar_tensor_tensor(a_g[1][:, m - 1, :], xT[:, m - 1, :], g_pe[:, l, m - 1:m],
                                                       a_g[0][:, m - 1, :], ALU.mult, ALU.subtract
                                                       ).then_inc(act_ready, 1)
                    before = link
                norm(3 * l + 1)
                for m in range(KT):
                    s = STEP_GATE[l] + m
                    dve.wait_ge(pj_done, s + 1)
                    nc.vector.tensor_tensor(t_a[m % 2][:], ps_pj[s % 2][:], rs[:], ALU.mult
                                            ).then_inc(pj_free[s % 2], 1)
                    dve.wait_ge(g_tanh, KT * l + m + 1)
                    link = chain(nc.vector.scalar_tensor_tensor(t_a[m % 2][:], t_b[m % 2][:], 1.0, pleT[:, m, :],
                                                                ALU.add, ALU.mult))
                    dve.wait_ge(v_self, link)
                    nc.vector.scalar_tensor_tensor(xT[:, m, :], t_a[m % 2][:], 0.5, xT[:, m, :], ALU.mult, ALU.add
                                                   ).then_inc(x_new, 1)
                    if l == 0:
                        dve.wait_ge(act_hi_done, ACT_H[1] + m + 1)
                        nc.vector.scalar_tensor_tensor(a_h[1][:, m, :], xT[:, m, :], g_pre[:, 1, m:m + 1],
                                                       a_h[0][:, m, :], ALU.mult, ALU.subtract
                                                       ).then_inc(act_ready, 1)
                if l == 1:
                    continue
                norm(2)
                nc.vector.memset(cv_w[:, 0:TAPS - 1], 0.0).then_inc(cv_pad, 1)
                link = chain(nc.vector.tensor_tensor(rs2[:], rs[:], rs[:], ALU.mult))
                dve.wait_ge(v_self, link)
                dve.wait_ge(cv_pad, 1)
                dve.wait_ge(g_loaded[4], 16)
                with dve.Fori(0, KT) as m:
                    s = [STEP_CONV + j for j in range(4)]
                    bank = [ps_pj[i % 2] for i in s]
                    dve.wait_ge(pj_done, 4 * m + s[0] + 1)
                    nc.vector.tensor_tensor(cv_c[:], bank[0][:], rs2[:], ALU.mult).then_inc(pj_free[s[0] % 2], 1)
                    dve.wait_ge(pj_free[s[0] % 2], 2 * m + s[0] // 2 + 1)
                    dve.wait_ge(pj_done, 4 * m + s[1] + 1)
                    nc.vector.tensor_tensor(cv_w[:, TAPS - 1:TAPS - 1 + SEQ], bank[1][:], cv_c[:], ALU.mult
                                            ).then_inc(pj_free[s[1] % 2], 1)
                    dve.wait_ge(pj_free[s[1] % 2], 2 * m + s[1] // 2 + 1)
                    nc.vector.tensor_scalar(cv_y[0][:], cv_w[:, 2:2 + SEQ], taps[:, 2, bass.ds(m, 1)], None, ALU.mult
                                            ).then_inc(cv_self, 1)
                    dve.wait_ge(cv_self, 6 * m + 1)
                    nc.vector.scalar_tensor_tensor(cv_y[1][:], cv_w[:, 1:1 + SEQ], taps[:, 1, bass.ds(m, 1)],
                                                   cv_y[0][:], ALU.mult, ALU.add).then_inc(cv_self, 1)
                    dve.wait_ge(cv_self, 6 * m + 2)
                    nc.vector.scalar_tensor_tensor(cv_y[0][:], cv_w[:, 0:SEQ], taps[:, 0, bass.ds(m, 1)],
                                                   cv_y[1][:], ALU.mult, ALU.add).then_inc(cv_self, 1)
                    dve.wait_ge(cv_self, 6 * m + 3)
                    dve.wait_ge(pj_done, 4 * m + s[2] + 1)
                    nc.vector.tensor_tensor(cv_y[1][:], bank[2][:], cv_y[0][:], ALU.mult
                                            ).then_inc(pj_free[s[2] % 2], 1)
                    dve.wait_ge(pj_done, 4 * m + s[3] + 1)
                    nc.vector.tensor_tensor(cv_z[:], bank[3][:], rs[:], ALU.mult).then_inc(pj_free[s[3] % 2], 1)
                    dve.wait_ge(cz_tanh, m + 1)
                    nc.vector.scalar_tensor_tensor(cv_t[:], cv_t[:], 1.0, cv_z[:], ALU.add, ALU.mult
                                                   ).then_inc(cv_self, 1)
                    dve.wait_ge(cv_self, 6 * m + 4)
                    nc.vector.scalar_tensor_tensor(cv_t[:], cv_t[:], 0.5, rs[:], ALU.mult, ALU.mult
                                                   ).then_inc(cv_self, 1)
                    dve.wait_ge(cv_self, 6 * m + 5)
                    nc.vector.tensor_tensor(cv_z[:], cv_y[1][:], cv_t[:], ALU.mult).then_inc(cv_self, 1)
                    dve.wait_ge(act_hi_done, m + ACT_U[1] + 1)
                    tile = bass.ds(m, 1)
                    nc.vector.tensor_tensor(act_lo[0][:, tile, :], cv_z[:].rearrange("p (o c) -> p o c", o=1),
                                            act_hi[0][:, tile, :], ALU.subtract).then_inc(act_ready, 1)

        @block.tensor
        def _(pe):
            def products(bank, place, a, ks, first, last, w=None):
                for k in ks:
                    w_h = w_hi[place % RING][:, k, :] if w is None else w[k][0]
                    w_l = w_lo[place % RING][:, k, :] if w is None else w[k][1]
                    nc.tensor.matmul(bank[:], w_h, a[0][:, k, :], start=k == first, stop=False)
                    nc.tensor.matmul(bank[:], w_h, a[1][:, k, :], start=False, stop=False)
                    end = nc.tensor.matmul(bank[:], w_l, a[0][:, k, :], start=False, stop=k == last)
                return end

            act0, act1 = (act_hi[0], act_lo[0]), (act_hi[1], act_lo[1])

            def transposes(n, tiles, done=tr_done):
                for t, tile in enumerate(tiles):
                    last = nc.tensor.transpose(ps_tr[n % 2][:, t * P:(t + 1) * P], tile, ident[:])
                last.then_inc(done, 1)

            pe.wait_ge(consts, 3)
            pe.wait_ge(x_norm, TT)
            for k in range(KT):
                if k >= 2:
                    pe.wait_ge(act_ready, k - 1)
                transposes(k, [x_n[:, t, k * P:(k + 1) * P] for t in range(TT)], xn_done)
            pe.wait_ge(w_ready, SLOT_F + 1)
            for k in range(KT):
                pe.wait_ge(act_ready, k + 1)
                end = products(ps_pj[0], 0, act0, [k], 0, KT - 1)
            end.then_inc(pj_done, 1)

            def turn(m0, jj, project, attend):
                b = m0 % 2
                for g in range(GROUPS):
                    j = g // 4
                    s = STEP_QKVZ + 4 * m0 + j
                    if project:
                        if g % 4 == 0:
                            pe.wait_ge(w_ready, count(SLOT_QKVZ + j + 1, 4, m0, jj))
                            wait(pe, pj_free[s % 2], halved(STEP_QKVZ + j, 4, m0, jj))
                        k = 2 * (g % 4)
                        end = products(ps_pj[s % 2], s, act0, [k, k + 1], 0, KT - 1)
                        if g % 4 == 3:
                            end.then_inc(pj_done, 1)
                    if attend and g in SCORE_AT:
                        u = SCORE_AT[g]
                        h, i = u // TT, u % TT
                        if g == 0:
                            sk = STEP_QKVZ + 4 * (m0 - 1) + 1
                            pe.wait_ge(pj_free[sk % 2], halved(STEP_QKVZ - 3 + 2, 4, m0, jj))
                        wait(pe, logit_ready, count(u - 8 - 1, 8, m0, jj))
                        queries, keys = slice(i * P, (i + 1) * P), slice(0, (i + 1) * P)
                        nc.tensor.matmul(ps_sc[u % 2][:, keys], q_hi[1 - b][h][:, queries], k_st[1 - b][h][:, keys],
                                         start=True, stop=False)
                        nc.tensor.matmul(ps_sc[u % 2][:, keys], q_lo[1 - b][h][:, queries], k_st[1 - b][h][:, keys],
                                         start=False, stop=True).then_inc(sc_done, 1)
                    if attend and g in TRANSPOSE_AT:
                        u = TRANSPOSE_AT[g]
                        n = USE_T + 9 * m0 + u
                        pe.wait_ge(prob_ready, count(u + 1 - 8, 8, m0, jj))
                        wait(pe, tr_free[n % 2], halved(USE_T + u, 9, m0, jj))
                        transposes(n, [logit[u % LOGIT_BUFS][:, k * P:(k + 1) * P] for k in range(u % TT + 1)])
                    if attend and g in PV_AT:
                        h = PV_AT[g]
                        n = USE_T + 9 * m0 + 4 * h + 3
                        pe.wait_ge(tr_free[n % 2], halved(USE_T + 4 * h + 3, 9, m0, jj) + 1)
                        wait(pe, o_free, count(h + 1 - 4, 2, m0, jj))
                        for k in range(TT):
                            cols = slice(k * PT_STEP + k * P, k * PT_STEP + SEQ)
                            v = v_st[:, k, h * P:(h + 1) * P]
                            nc.tensor.matmul(ps_o[h][:, k * P:SEQ], v, pt_hi[:, cols], start=k == 0, stop=False)
                            last = nc.tensor.matmul(ps_o[h][:, k * P:SEQ], v, pt_lo[:, cols], start=False,
                                                    stop=k == TT - 1)
                        last.then_inc(pv_done, 1)
                    if g == GROUPS - 1 and project:
                        n, sv = USE_V + 9 * m0, STEP_QKVZ + 4 * m0 + 2
                        pe.wait_ge(pj_free[sv % 2], halved(STEP_QKVZ + 2, 4, m0, jj) + 1)
                        wait(pe, tr_free[n % 2], halved(USE_V, 9, m0, jj))
                        transposes(n, [vT[:, t * P:(t + 1) * P] for t in range(TT)])

            turn(0, 0, True, False)
            turn(1, 0, True, True)
            with pe.Fori(0, (PAIRS - 2) // 2) as jj:
                turn(2, jj, True, True)
                turn(3, jj, True, True)
            turn(PAIRS, 0, False, True)

            def step(s, slot, a, tiles):
                pe.wait_ge(w_ready, slot + 1)
                pe.wait_ge(pj_free[s % 2], s // 2)
                for k in range(KT):
                    pe.wait_ge(act_ready, tiles + k + 1)
                    end = products(ps_pj[s % 2], slot, a, [k], 0, KT - 1)
                end.then_inc(pj_done, 1)

            def norm(n):
                pe.wait_ge(acc_ready, n + 1)
                pe.wait_ge(mean_ready, 2)
                wait(pe, root_done, n)
                nc.tensor.matmul(ps_o[0][:], mean_w[:], acc_hi[:], start=True, stop=False)
                nc.tensor.matmul(ps_o[0][:], mean_w[:], acc_lo[:], start=False, stop=True).then_inc(st_done, 1)

            for l in range(2):
                a_u, a_g = (act1, act0) if l == 0 else (act0, act1)
                for m in range(KT):
                    step(STEP_OUT[l] + m, SLOT_OUT[l] + m, a_u, ACT_U[l])
                norm(3 * l)
                pe.wait_ge(p_ready, l + 1)
                pe.wait_ge(w_ready, SLOT_PLE[l] + PLE_KT)
                for m in range(KT):
                    s = STEP_PLE[l] + m
                    pe.wait_ge(pj_free[s % 2], s // 2)
                    w = [(w_hi[(SLOT_PLE[l] + k) % RING][:, m, :], w_lo[(SLOT_PLE[l] + k) % RING][:, m, :])
                         for k in range(PLE_KT)]
                    end = products(ps_pj[s % 2], 0, (p_hi, p_lo), range(PLE_KT), 0, PLE_KT - 1, w)
                    end.then_inc(pj_done, 1)
                for m in range(KT):
                    step(STEP_GATE[l] + m, SLOT_GATE[l] + m, a_g, ACT_G[l])
                    if m == 0:
                        norm(3 * l + 1)
                if l == 0:
                    norm(2)
                    with pe.Fori(0, KT) as m:
                        for j in range(4):
                            s, slot = STEP_CONV + j, SLOT_CONV + j
                            pe.wait_ge(w_ready, 4 * m + slot + 1)
                            pe.wait_ge(pj_free[s % 2], 2 * m + s // 2)
                            pe.wait_ge(act_ready, ACT_H[1] + KT)
                            end = products(ps_pj[s % 2], slot, act1, range(KT), 0, KT - 1)
                            end.then_inc(pj_done, 1)


def slots(w):
    n = w.shape[1] // P
    return w.reshape(KT, P, n, P).transpose(2, 1, 0, 3).reshape(n, P, D)


def weight_stream(attn_w_in, attn_w_out, conv_w_in, conv_w_out, pe_w_gate, pe_w_proj):
    f = np.zeros((D, P), attn_w_in.dtype)
    f[:, :HEADS] = attn_w_in[0][:, 4 * D:]
    qkvz = slots(attn_w_in[0][:, :4 * D]).reshape(4, PAIRS, P, D).transpose(1, 0, 2, 3).reshape(4 * PAIRS, P, D)
    bchz = slots(conv_w_in[0]).reshape(4, KT, P, D)
    chbz = bchz[[1, 2, 0, 3]].transpose(1, 0, 2, 3).reshape(4 * KT, P, D)
    tails = [[slots(w[0]), pe_w_proj[i].reshape(PLE_KT, P, D), slots(pe_w_gate[i])]
             for i, w in enumerate((attn_w_out, conv_w_out))]
    return np.concatenate([slots(f), qkvz, *tails[0], chbz, *tails[1]])


def kernel(**inputs):
    import concourse.bacc as bacc
    from concourse.bass_utils import run_bass_kernel_spmd

    a = {name: np.asarray(value) for name, value in inputs.items()}
    by_feature = lambda v: v.reshape(-1, KT, P).transpose(2, 0, 1)
    arrays = {
        "in_x": a["x"][0],
        "in_xT": a["x"][0].T.reshape(KT, P, SEQ),
        "in_pT": a["p"][:, 0].transpose(0, 2, 1).reshape(2, PLE_KT, P, SEQ).transpose(0, 2, 1, 3),
        "in_weights": weight_stream(a["attn_w_in"], a["attn_w_out"], a["conv_w_in"], a["conv_w_out"],
                                    a["pe_w_gate"], a["pe_w_proj"]),
        "in_b_f": a["attn_b_f"].reshape(HEADS, 1),
        "in_norm_pre": by_feature(a["norm_pre"]),
        "in_norm_post": by_feature(a["norm_post"]),
        "in_pe_norm": by_feature(a["pe_norm"]),
        "in_taps": by_feature(a["conv_kernel"][0]),
    }
    arrays = {name: np.ascontiguousarray(value) for name, value in arrays.items()}
    nc = bacc.Bacc("TRN2", target_bir_lowering=False, num_devices=1)
    args = [nc.dram_tensor(name, v.shape, mybir.dt.from_np(v.dtype), kind="ExternalInput").ap()
            for name, v in arrays.items()]
    out = nc.dram_tensor("out_0", (KT, P, SEQ), F32, kind="ExternalOutput").ap()
    trunk(nc, *args, out)
    result = run_bass_kernel_spmd(nc, [arrays], core_ids=[0])
    return result.results[0]["out_0"].reshape(D, SEQ).T.reshape(1, SEQ, D)
```

```python
from contextlib import ExitStack

import numpy as np
import concourse.bass as bass
from concourse import mybir

F32 = mybir.dt.float32
F32R = mybir.dt.float32r
ALU = mybir.AluOpType
ACT = mybir.ActivationFunctionType

P = 128
SEQ = 512
D = 1024
KT = D // P
TT = SEQ // P
HEADS = 16
DH = D // HEADS
PAIRS = HEADS // 2
PLE = 256
PLE_KT = PLE // P
TAPS = 3
EPS = 1e-6
MASKED = -1e30
RING = 4
RAW = 2
LOGIT_BUFS = 4
PT_STEP = (TT - 1) * P
PLE_STEPS = KT // 2

STEP_F = 0
STEP_QKVZ = 1
TAIL_STEPS = 2 * KT + PLE_STEPS
STEP_OUT = [STEP_QKVZ + 4 * PAIRS, STEP_QKVZ + 4 * PAIRS + TAIL_STEPS + 4 * KT]
STEP_PLE = [s + KT for s in STEP_OUT]
STEP_GATE = [s + KT + PLE_STEPS for s in STEP_OUT]
STEP_CONV = STEP_OUT[0] + TAIL_STEPS
SLOT_F = 0
SLOT_QKVZ = 1
TAIL_SLOTS = 2 * KT + PLE_KT
SLOT_OUT = [SLOT_QKVZ + 4 * PAIRS, SLOT_QKVZ + 4 * PAIRS + TAIL_SLOTS + 4 * KT]
SLOT_PLE = [s + KT for s in SLOT_OUT]
SLOT_GATE = [s + KT + PLE_KT for s in SLOT_OUT]
SLOT_CONV = SLOT_OUT[0] + TAIL_SLOTS
SLOTS = SLOT_OUT[1] + TAIL_SLOTS
TR_BANKS = 3
USE_V = 0
USE_T = -8
ACT_H = [0, 3 * KT]
ACT_U = [KT, 4 * KT]
ACT_G = [2 * KT, 5 * KT]
SCORE_AT = {0: 0, 1: 1, 2: 2, 3: 3, 6: 4, 7: 5, 8: 6, 9: 7}
TRANSPOSE_AT = {3: 0, 4: 1, 5: 2, 6: 3, 9: 4, 10: 5, 11: 6, 12: 7}
PV_AT = {8: 0, 13: 1}
SUM_AT = {9: 0, 14: 1}
WEIGHTS_AT = 2
V_AT = 14
GROUPS = 16


def wait(eng, sem, count):
    if not isinstance(count, int) or count > 0:
        eng.wait_ge(sem, count)


def trunk(nc, x, xT_in, pT_in, weights, b_f_in, pre_in, post_in, pe_in, taps_in, outT):
    negc_dram = nc.dram_tensor("negc_scratch", [HEADS, SEQ], F32).ap()

    ctx = ExitStack()
    with ctx:
        def sb(name, shape, dt=F32, at=ctx):
            return at.enter_context(nc.sbuf_tensor(name, shape, dt))

        def sem(name):
            return ctx.enter_context(nc.semaphore(name))

        xT = sb("xT", [P, KT, SEQ])
        act_hi = [sb(f"act{i}_hi", [P, KT, SEQ], F32R) for i in range(2)]
        act_lo = [sb(f"act{i}_lo", [P, KT, SEQ], F32R) for i in range(2)]
        w_raw = [sb(f"w_raw{i}", [P, KT, P]) for i in range(RAW)]
        w_hi = [sb(f"w_hi{i}", [P, KT, P], F32R) for i in range(RING)]
        w_lo = [sb(f"w_lo{i}", [P, KT, P], F32R) for i in range(RING)]
        ident = sb("ident", [P, P])
        future = sb("future", [P, P])
        mean_f = sb("mean_f", [P, P])
        mean_w = sb("mean_w", [P, P], F32R)
        g_pre = sb("g_pre", [P, 2, KT])
        g_post = sb("g_post", [P, 2, KT])
        g_pe = sb("g_pe", [P, 2, KT])
        taps = sb("taps", [P, TAPS, KT])
        ss = sb("ss", [P, TT])
        rms = sb("rms", [P, TT])
        rinv = sb("rinv", [P, TT])
        b_f = sb("b_f", [HEADS, 1])
        gap = sb("gap", [P, LOGIT_BUFS])
        nmax = sb("nmax", [P, LOGIT_BUFS])
        rsum = sb("rsum", [P, LOGIT_BUFS])
        rrec = sb("rrec", [P, LOGIT_BUFS])
        start = ExitStack()
        x_in = sb("x_in", [P, TT, D], at=start)
        f_part = ExitStack()
        ones_f = sb("ones_f", [HEADS, SEQ], at=f_part)
        f_x = sb("f_x", [HEADS, SEQ], at=f_part)
        f_abs = sb("f_abs", [HEADS, SEQ], at=f_part)
        f_ln = sb("f_ln", [HEADS, SEQ], at=f_part)
        f_negc = sb("f_negc", [HEADS, SEQ], at=f_part)
        f_part.close()
        x_n = sb("x_n", [P, TT, D], at=start)
        start.close()
        attn = ExitStack()
        logit = [sb(f"logit{i}", [P, SEQ], at=attn) for i in range(LOGIT_BUFS)]
        pt_hi = sb("pt_hi", [P, TT * PT_STEP + PT_STEP], F32R, attn)
        pt_lo = sb("pt_lo", [P, TT * PT_STEP + PT_STEP], F32R, attn)
        o_half = sb("o_half", [P, SEQ], at=attn)
        o_u = sb("o_u", [P, SEQ], at=attn)
        v_st = sb("v_st", [P, TT, 4 * DH], F32R, attn)
        vT = sb("vT", [P, SEQ], at=attn)
        z_tanh = sb("z_tanh", [P, SEQ], at=attn)
        z_silu = sb("z_silu", [P, SEQ], at=attn)
        q_hi = [[sb(f"q_hi{b}{h}", [P, SEQ], F32R, attn) for h in range(2)] for b in range(2)]
        q_lo = [[sb(f"q_lo{b}{h}", [P, SEQ], F32R, attn) for h in range(2)] for b in range(2)]
        k_st = [[sb(f"k_st{b}{h}", [P, SEQ], F32R, attn) for h in range(2)] for b in range(2)]
        bias = [sb(f"bias{h}", [P, TT, SEQ], at=attn) for h in range(2)]
        attn.close()
        late = ExitStack()
        conv = ExitStack()
        cv_c = sb("cv_c", [P, SEQ], at=conv)
        cv_w = sb("cv_w", [P, TAPS - 1 + SEQ], at=conv)
        cv_y = [sb(f"cv_y{i}", [P, SEQ], at=conv) for i in range(2)]
        cv_z = sb("cv_z", [P, SEQ], at=conv)
        cv_t = sb("cv_t", [P, SEQ], at=conv)
        conv.close()
        yT = sb("yT", [P, KT, SEQ], at=late)
        pleT = sb("pleT", [P, PLE_STEPS, SEQ], at=late)
        p_in = sb("p_in", [P, PLE_KT, SEQ], at=late)
        p_hi = sb("p_hi", [P, PLE_KT, SEQ], F32R, late)
        p_lo = sb("p_lo", [P, PLE_KT, SEQ], F32R, late)
        sq = [sb(f"sq{i}", [P, SEQ], at=late) for i in range(2)]
        acc = sb("acc", [P, SEQ], at=late)
        acc_hi = sb("acc_hi", [P, SEQ], F32R, late)
        acc_lo = sb("acc_lo", [P, SEQ], F32R, late)
        rs_root = sb("rs_root", [P, SEQ], at=late)
        rs = sb("rs", [P, SEQ], at=late)
        rs2 = sb("rs2", [P, SEQ], at=late)
        t_a = [sb(f"t_a{i}", [P, SEQ], at=late) for i in range(2)]
        t_b = [sb(f"t_b{i}", [P, SEQ], at=late) for i in range(2)]
        late.close()

        ps_pj = [ctx.enter_context(nc.psum_tensor(f"ps_pj{i}", [P, SEQ], F32)) for i in range(2)]
        ps_sc = [ctx.enter_context(nc.psum_tensor(f"ps_sc{i}", [P, SEQ], F32)) for i in range(2)]
        ps_tr = [ctx.enter_context(nc.psum_tensor(f"ps_tr{i}", [P, SEQ], F32)) for i in range(TR_BANKS)]
        ps_o = ctx.enter_context(nc.psum_tensor("ps_o", [P, SEQ], F32))
        ps_ple = [ps_sc[0], ps_sc[1], ps_tr[0], ps_tr[1]]

        x_loaded = [sem(f"x_loaded{t}") for t in range(TT)]
        g_loaded = [sem(f"g_loaded{i}") for i in range(5)]
        p_loaded = sem("p_loaded")
        w_loaded = [sem(f"w_loaded{i}") for i in range(RAW)]
        res_loaded = sem("res_loaded")
        w_hi_done = sem("w_hi_done")
        w_ready = sem("w_ready")
        pj_done = sem("pj_done")
        pj_free = [sem(f"pj_free{i}") for i in range(2)]
        xn_done = sem("xn_done")
        tr_done = sem("tr_done")
        tr_free = [sem(f"tr_free{i}") for i in range(TR_BANKS)]
        consts = sem("consts")
        mean_ready = sem("mean_ready")
        x_ss = sem("x_ss")
        x_root = sem("x_root")
        x_rinv = sem("x_rinv")
        x_norm = sem("x_norm")
        act_hi_done = sem("act_hi_done")
        act_ready = sem("act_ready")
        f_chain = sem("f_chain")
        f_act = sem("f_act")
        negc_stored = sem("negc_stored")
        bias_loaded = [sem(f"bias_loaded{h}") for h in range(2)]
        bias_ready = [sem(f"bias_ready{h}") for h in range(2)]
        q_hi_done = sem("q_hi_done")
        k_hi_done = sem("k_hi_done")
        v_hi_done = sem("v_hi_done")
        z_tanh_done = sem("z_tanh_done")
        sc_done = sem("sc_done")
        logit_ready = sem("logit_ready")
        exp_done = sem("exp_done")
        rec_done = sem("rec_done")
        prob_ready = sem("prob_ready")
        pt_hi_done = sem("pt_hi_done")
        pv_done = sem("pv_done")
        o_half_done = sem("o_half_done")
        o_free = sem("o_free")
        u_ready = sem("u_ready")
        p_hi_done = sem("p_hi_done")
        p_ready = sem("p_ready")
        sq_ready = sem("sq_ready")
        acc_done = sem("acc_done")
        acc_hi_done = sem("acc_hi_done")
        acc_ready = sem("acc_ready")
        st_done = sem("st_done")
        root_done = sem("root_done")
        rs_ready = sem("rs_ready")
        x_new = sem("x_new")
        y_scaled = sem("y_scaled")
        v_self = sem("v_self")
        g_tanh = sem("g_tanh")
        cv_pad = sem("cv_pad")
        cv_self = sem("cv_self")
        cz_tanh = sem("cz_tanh")
        stored = sem("stored")

        block = ctx.enter_context(nc.Block())

        def count(c, per, m0, jj):
            return c + per * m0 + 2 * per * jj

        def halved(c, per, m0, jj):
            return (c + per * m0) // 2 + per * jj

        def tr_uses(c, m0, jj):
            return c // TR_BANKS + 9 // TR_BANKS * (m0 + 2 * jj)

        def last_step(slot):
            for l in range(2):
                if SLOT_PLE[l] <= slot < SLOT_GATE[l]:
                    return STEP_GATE[l] - 1
            passed = sum(slot >= SLOT_GATE[l] for l in range(2))
            return slot + passed * (PLE_STEPS - PLE_KT)

        def causal(pt, i):
            part = pt[:, i * P:i * P + PT_STEP * (i + 1)]
            return part.rearrange("p (k c) -> p k c", c=PT_STEP)[:, :, 0:P]

        @block.sync
        def _(sp):
            def load_slot(slot, place):
                wait(sp, w_ready, slot - RAW + 1)
                src = weights[bass.ds(slot, 1), :, :].rearrange("o p (k c) -> p (o k) c", c=P)
                sp.dma_start(w_raw[place % RAW][:], src).then_inc(w_loaded[place % RAW], 16)

            def load_bias(a, h):
                wait(sp, logit_ready, 8 * a - 8 + 4 * h + 4)
                for i in range(TT):
                    n = (i + 1) * P
                    row = negc_dram[bass.ds(2 * a + h, 1), 0:n]
                    sp.dma_start(bias[h][:, i, 0:n], row.to_broadcast([P, n])).then_inc(bias_loaded[h], 16)

            for t in range(TT):
                sp.dma_start(x_in[:, t, :], x[t * P:(t + 1) * P, :]).then_inc(x_loaded[t], 16)
                if t == 1:
                    load_slot(0, 0)
            sp.dma_start(g_pre[:], pre_in).then_inc(g_loaded[0], 16)
            sp.dma_start(b_f[:], b_f_in).then_inc(g_loaded[1], 16)
            for slot in range(1, 6):
                load_slot(slot, slot)
            sp.dma_start(g_post[:], post_in).then_inc(g_loaded[2], 16)
            sp.dma_start(g_pe[:], pe_in).then_inc(g_loaded[3], 16)
            sp.dma_start(taps[:], taps_in).then_inc(g_loaded[4], 16)
            sp.wait_ge(f_chain, 3)
            sp.dma_start(negc_dram, f_negc[:]).then_inc(negc_stored, 16)
            sp.wait_ge(negc_stored, 16)

            def turn(m):
                load_slot(6 + 4 * m, 6)
                load_bias(m, 0)
                load_slot(7 + 4 * m, 7)
                load_slot(8 + 4 * m, 8)
                load_bias(m, 1)
                load_slot(9 + 4 * m, 9)

            turn(0)
            sp.dma_start(xT[:], xT_in.rearrange("k p t -> p k t")).then_inc(res_loaded, 16)
            with sp.Fori(1, PAIRS) as m:
                turn(m)
            for slot in range(6 + 4 * PAIRS, SLOT_CONV + RAW):
                load_slot(slot, slot)
                if slot == 7 + 4 * PAIRS:
                    sp.wait_ge(act_ready, ACT_U[0] + KT)
                    sp.dma_start(p_in[:], pT_in[0]).then_inc(p_loaded, 16)
            with sp.Fori(0, KT) as m:
                for j in range(4):
                    load_slot(4 * m + SLOT_CONV + RAW + j, SLOT_CONV + RAW + j)
            sp.wait_ge(p_ready, 1)
            sp.dma_start(p_in[:], pT_in[1]).then_inc(p_loaded, 16)
            for slot in range(SLOT_OUT[1] + RAW, SLOTS):
                load_slot(slot, slot)
            for m in range(KT):
                sp.wait_ge(x_new, 3 * KT + m + 1)
                sp.dma_start(outT[m], xT[:, m, :]).then_inc(stored, 16)
            sp.wait_ge(stored, 16 * KT)

        @block.gpsimd
        def _(pool):
            nc.gpsimd.memset(ident[:], 0.0).then_inc(consts, 1)
            pool.wait_ge(consts, 1)
            nc.gpsimd.affine_select(out=ident[:], in_=ident[:], compare_op=ALU.not_equal, fill=1.0, base=0,
                                    pattern=[[-1, P]], channel_multiplier=1).then_inc(consts, 1)
            nc.gpsimd.memset(mean_f[:], 1.0 / D).then_inc(consts, 1)
            nc.gpsimd.memset(future[:], 0.0).then_inc(consts, 1)
            pool.wait_ge(consts, 4)
            nc.gpsimd.affine_select(out=future[:], in_=future[:], compare_op=ALU.is_ge, fill=MASKED, base=0,
                                    pattern=[[-1, P]], channel_multiplier=1).then_inc(consts, 1)
            pool.wait_ge(consts, 5)

            def weight_lo(slot, place):
                pool.wait_ge(w_hi_done, slot + 1)
                nc.gpsimd.tensor_tensor(w_lo[place % RING][:], w_raw[place % RAW][:], w_hi[place % RING][:],
                                        ALU.subtract).then_inc(w_ready, 1)

            def mask(a, h):
                pool.wait_ge(bias_loaded[h], 64 * a + 64)
                for i in range(TT):
                    diagonal = bias[h][:, i, i * P:(i + 1) * P]
                    nc.gpsimd.tensor_tensor(diagonal, diagonal, future[:], ALU.add).then_inc(bias_ready[h], 1)

            def turn(m):
                weight_lo(4 + 4 * m, 4)
                weight_lo(5 + 4 * m, 5)
                mask(m, 0)
                weight_lo(6 + 4 * m, 6)
                weight_lo(7 + 4 * m, 7)
                mask(m, 1)

            for slot in range(4):
                weight_lo(slot, slot)
            with pool.Fori(0, PAIRS) as m:
                turn(m)

            def add_square(n):
                pool.wait_ge(sq_ready, n + 1)
                if n % KT == 0:
                    wait(pool, acc_ready, n // KT)
                    nc.gpsimd.tensor_copy(acc[:], sq[n % 2][:]).then_inc(acc_done, 1)
                else:
                    pool.wait_ge(acc_done, n)
                    nc.gpsimd.tensor_tensor(acc[:], acc[:], sq[n % 2][:], ALU.add).then_inc(acc_done, 1)

            for l in range(2):
                for m in range(KT):
                    weight_lo(SLOT_OUT[l] + m + 3, SLOT_OUT[l] + m + 3)
                    add_square(3 * KT * l + m)
                weight_lo(SLOT_GATE[l] + 1, SLOT_GATE[l] + 1)
                pool.wait_ge(rs_ready, 3 * l + 1)
                for m in range(KT):
                    for tile in ([0, 2] if m == 0 else [m + 2] if m % 2 == 0 and m + 2 < KT else []):
                        wait(pool, x_new, 2 * KT * l + tile - 1)
                        nc.gpsimd.tensor_tensor(t_a[0][:], yT[:, tile, :], rs[:], ALU.mult).then_inc(y_scaled, 1)
                    add_square(3 * KT * l + KT + m)
                weight_lo(SLOT_GATE[l] + 2, SLOT_GATE[l] + 2)
                for m in range(KT):
                    if SLOT_GATE[l] + m + 3 < SLOTS:
                        weight_lo(SLOT_GATE[l] + m + 3, SLOT_GATE[l] + m + 3)
                    if l == 0:
                        add_square(2 * KT + m)
                if l == 0:
                    with pool.Fori(0, KT) as m:
                        for j in range(4):
                            weight_lo(4 * m + SLOT_CONV + 3 + j, SLOT_CONV + 3 + j)

        @block.scalar
        def _(act):
            def weight_hi(slot, place):
                act.wait_ge(w_loaded[place % RAW], 16 * (place // RAW + 1) + (16 // RAW) * (slot - place))
                if place >= RING:
                    act.wait_ge(pj_done, last_step(place - RING) + 1 + (slot - place))
                nc.scalar.copy(w_hi[place % RING][:], w_raw[place % RAW][:]).then_inc(w_hi_done, 1)

            for t in range(TT):
                act.wait_ge(x_loaded[t], 16)
                nc.scalar.activation(x_n[:, t, :], x_in[:, t, :], ACT.Square, accum_out=ss[:, t:t + 1]).then_inc(x_ss, 1)
                act.wait_ge(x_ss, t + 1)
                nc.scalar.activation(rms[:, t:t + 1], ss[:, t:t + 1], ACT.Sqrt, scale=1.0 / D,
                                     bias=EPS).then_inc(x_root, 1)
            act.wait_ge(g_loaded[0], 16)
            weight_hi(0, 0)
            for k in range(KT):
                act.wait_ge(xn_done, k + 1)
                nc.scalar.activation(act_hi[0][:, k, :], ps_tr[k % TR_BANKS][:], ACT.Copy,
                                     scale=g_pre[:, 0, k:k + 1]).then_inc(act_hi_done, 1)
                if k % 2 == 1 and k < 6:
                    weight_hi((k + 1) // 2, (k + 1) // 2)

            def score_exp(u, m0, jj):
                act.wait_ge(logit_ready, count(u + 1 - 8, 8, m0, jj))
                b, n = u % LOGIT_BUFS, (u % TT + 1) * P
                nc.scalar.activation(logit[b][:, 0:n], logit[b][:, 0:n], ACT.Exp, scale=-1.0, bias=nmax[:, b:b + 1],
                                     accum_out=rsum[:, b:b + 1]).then_inc(exp_done, 1)

            def pt_round(u, m0, jj):
                n = USE_T + 9 * m0 + u
                act.wait_ge(tr_done, count(USE_T + u + 1, 9, m0, jj))
                if u % TT == 0:
                    wait(act, pv_done, count(u // TT - 2, 2, m0, jj))
                i = u % TT
                nc.scalar.copy(causal(pt_hi, i), ps_tr[n % TR_BANKS][:, 0:(i + 1) * P].rearrange("p (k c) -> p k c", c=P)
                               ).then_inc(pt_hi_done, 1)

            def head_half(h, m0, jj):
                act.wait_ge(pv_done, count(h - 1, 2, m0, jj))
                wait(act, o_free, count(h + 1 - 4, 2, m0, jj))
                own, other = slice(h * DH, h * DH + DH), slice(DH - h * DH, 2 * DH - h * DH)
                nc.scalar.copy(o_half[own, :], ps_o[other, :]).then_inc(o_half_done, 1)

            def turn(m0, jj, project, attend):
                m = m0 + 2 * jj
                b = m0 % 2
                s = STEP_QKVZ + 4 * m0
                for g in range(GROUPS):
                    if attend and g in TRANSPOSE_AT:
                        pt_round(TRANSPOSE_AT[g], m0, jj)
                    if attend and g in SCORE_AT:
                        score_exp(SCORE_AT[g], m0, jj)
                    if g == 0 and attend:
                        act.wait_ge(pj_done, count(STEP_QKVZ, 4, m0, jj))
                        nc.scalar.activation(z_tanh[:], ps_pj[(s - 1) % 2][:], ACT.Tanh, scale=0.5
                                             ).then_inc(z_tanh_done, 1)
                    if g in (4, 5) and project:
                        h = g - 4
                        act.wait_ge(pj_done, count(STEP_QKVZ + 1, 4, m0, jj))
                        for r in range(2):
                            last = nc.scalar.mul(q_hi[b][h][r * DH:r * DH + DH, :],
                                                 ps_pj[s % 2][h * DH:h * DH + DH, :], DH ** -0.5)
                        last.then_inc(q_hi_done, 1)
                    if g == 8 and project:
                        act.wait_ge(pj_done, count(STEP_QKVZ + 2, 4, m0, jj))
                        for h in range(2):
                            own = slice(h * DH, h * DH + DH)
                            last = nc.scalar.copy(k_st[b][h][own, :], ps_pj[(s + 1) % 2][own, :])
                        last.then_inc(k_hi_done, 1)
                    if g == 12 and project:
                        act.wait_ge(pj_done, count(STEP_QKVZ + 3, 4, m0, jj))
                        nc.scalar.copy(vT[:], ps_pj[(s + 2) % 2][:]).then_inc(pj_free[(s + 2) % 2], 1)
                    if g % 4 == WEIGHTS_AT and project:
                        weight_hi(count(4 + g // 4, 4, m0, jj), 4 + 4 * m0 + g // 4)
                    if not attend and g == 0:
                        act.wait_ge(f_chain, 1)
                        nc.scalar.activation(f_ln[:], f_abs[:], ACT.Exp, scale=-1.0).then_inc(f_act, 1)
                        act.wait_ge(f_act, 1)
                        nc.scalar.activation(f_ln[:], f_ln[:], ACT.Ln, bias=1.0).then_inc(f_act, 1)
                    if attend and g in SUM_AT:
                        head_half(SUM_AT[g], m0, jj)
                    if g == V_AT and project:
                        n = USE_V
                        act.wait_ge(tr_done, count(USE_V + 1, 9, m0, jj))
                        wait(act, pv_done, count(0, 2, m0, jj))
                        dst = v_st[:].rearrange("p t (a b c) -> p t a b c", a=2, c=DH)
                        src = ps_tr[n % TR_BANKS][:].rearrange("p (t h c) -> p t h c", h=2, c=DH)
                        for h in range(2):
                            last = nc.scalar.copy(dst[:, :, h, h, :], src[:, :, h, :])
                        last.then_inc(v_hi_done, 1)
                    if attend and g == GROUPS - 1:
                        act.wait_ge(u_ready, m)
                        nc.scalar.copy(act_hi[1][:, bass.ds(m - 1, 1), :], o_u[:].rearrange("p (o c) -> p o c", o=1)
                                       ).then_inc(act_hi_done, 1)

            turn(0, 0, True, False)
            turn(1, 0, True, True)
            with act.Fori(0, (PAIRS - 2) // 2) as jj:
                turn(2, jj, True, True)
                turn(3, jj, True, True)
            turn(PAIRS, 0, False, True)

            def square(n, src):
                wait(act, acc_done, n - 1)
                nc.scalar.activation(sq[n % 2][:], src, ACT.Square).then_inc(sq_ready, 1)

            def norm(n):
                act.wait_ge(acc_done, KT * (n + 1))
                wait(act, st_done, n)
                nc.scalar.copy(acc_hi[:], acc[:]).then_inc(acc_hi_done, 1)
                if n % 3 == 0:
                    l = n // 3
                    weight_hi(SLOT_GATE[l] + 1, SLOT_GATE[l] + 1)
                act.wait_ge(st_done, n + 1)
                wait(act, rs_ready, n)
                nc.scalar.activation(rs_root[:], ps_o[:], ACT.Sqrt, bias=EPS).then_inc(root_done, 1)

            for l in range(2):
                a_g, a_h = act_hi[l], act_hi[1 - l]
                for m in range(KT):
                    weight_hi(SLOT_OUT[l] + m + 3, SLOT_OUT[l] + m + 3)
                    s = STEP_OUT[l] + m
                    act.wait_ge(pj_done, s + 1)
                    square(3 * KT * l + m, ps_pj[s % 2][:])
                    if m == 0:
                        act.wait_ge(g_loaded[2], 16)
                    nc.scalar.activation(yT[:, m, :], ps_pj[s % 2][:], ACT.Copy, scale=g_post[:, l, m:m + 1]
                                         ).then_inc(pj_free[s % 2], 1)
                    if m == 6:
                        act.wait_ge(p_loaded, 16 * l + 16)
                        nc.scalar.copy(p_hi[:], p_in[:]).then_inc(p_hi_done, 1)
                norm(3 * l)
                act.wait_ge(g_loaded[3], 16)
                for m in range(KT):
                    act.wait_ge(x_new, 2 * KT * l + m + 1)
                    nc.scalar.activation(a_g[:, m, :], xT[:, m, :], ACT.Copy, scale=g_pe[:, l, m:m + 1]
                                         ).then_inc(act_hi_done, 1)
                    square(3 * KT * l + KT + m, xT[:, m, :])
                    if m < PLE_STEPS:
                        s = STEP_PLE[l] + m
                        act.wait_ge(pj_done, s + 1)
                        nc.scalar.copy(pleT[:, m, :], ps_pj[s % 2][:]).then_inc(pj_free[s % 2], 1)
                weight_hi(SLOT_GATE[l] + 2, SLOT_GATE[l] + 2)
                norm(3 * l + 1)
                for m in range(KT):
                    if SLOT_GATE[l] + m + 3 < SLOTS:
                        weight_hi(SLOT_GATE[l] + m + 3, SLOT_GATE[l] + m + 3)
                    s = STEP_GATE[l] + m
                    act.wait_ge(pj_free[s % 2], s // 2 + 1)
                    nc.scalar.activation(t_b[m % 2][:], t_a[m % 2][:], ACT.Tanh, scale=0.5).then_inc(g_tanh, 1)
                    if l == 0:
                        act.wait_ge(x_new, KT + m + 1)
                        nc.scalar.activation(a_h[:, m, :], xT[:, m, :], ACT.Copy, scale=g_pre[:, 1, m:m + 1]
                                             ).then_inc(act_hi_done, 1)
                        square(2 * KT + m, xT[:, m, :])
                if l == 0:
                    norm(2)
                    with act.Fori(0, KT) as m:
                        for j in range(4):
                            slot = SLOT_CONV + 3 + j
                            weight_hi(4 * m + slot, slot)
                        sz = STEP_CONV + 3
                        act.wait_ge(pj_free[sz % 2], sz // 2 + 1 + 2 * m)
                        nc.scalar.activation(cv_t[:], cv_z[:], ACT.Tanh, scale=0.5).then_inc(cz_tanh, 1)
                        act.wait_ge(cv_self, 6 * m + 6)
                        nc.scalar.copy(act_hi[0][:, bass.ds(m, 1), :], cv_z[:].rearrange("p (o c) -> p o c", o=1)
                                       ).then_inc(act_hi_done, 1)

        @block.vector
        def _(dve):
            for t in range(TT):
                dve.wait_ge(x_root, t + 1)
                nc.vector.reciprocal(rinv[:, t:t + 1], rms[:, t:t + 1]).then_inc(x_rinv, 1)
                dve.wait_ge(x_rinv, t + 1)
                nc.vector.tensor_scalar(x_n[:, t, :], x_in[:, t, :], rinv[:, t:t + 1], None, ALU.mult
                                        ).then_inc(x_norm, 1)
            dve.wait_ge(g_loaded[0], 16)
            for k in range(KT):
                dve.wait_ge(act_hi_done, k + 1)
                nc.vector.scalar_tensor_tensor(act_lo[0][:, k, :], ps_tr[k % TR_BANKS][:], g_pre[:, 0, k:k + 1],
                                               act_hi[0][:, k, :], ALU.mult, ALU.subtract
                                               ).then_inc(act_ready, 1)
            dve.wait_ge(consts, 3)
            nc.vector.tensor_copy(mean_w[:], mean_f[:]).then_inc(mean_ready, 1)
            nc.vector.memset(ones_f[:], 1.0).then_inc(mean_ready, 1)
            dve.wait_ge(g_loaded[1], 16)
            dve.wait_ge(pj_done, STEP_F + 1)
            nc.vector.tensor_scalar(f_x[:], ps_pj[0][0:HEADS, :], b_f[:], None, ALU.add).then_inc(pj_free[0], 1)
            dve.wait_ge(pj_free[0], 1)
            nc.vector.scalar_tensor_tensor(f_abs[:], f_x[:], -1.0, f_x[:], ALU.mult, ALU.max).then_inc(f_chain, 1)
            dve.wait_ge(f_act, 2)
            nc.vector.scalar_tensor_tensor(f_x[:], f_x[:], 0.0, f_ln[:], ALU.min, ALU.subtract).then_inc(f_chain, 1)
            dve.wait_ge(mean_ready, 2)
            dve.wait_ge(f_chain, 2)
            nc.vector.tensor_tensor_scan(f_negc[:], ones_f[:], f_x[:], 0.0, ALU.mult, ALU.subtract
                                         ).then_inc(f_chain, 1)

            def score_logits(u, m0, jj):
                h, i, b, n = u // TT, u % TT, u % LOGIT_BUFS, (u % TT + 1) * P
                dve.wait_ge(sc_done, count(u + 1 - 8, 8, m0, jj))
                if i == 0:
                    dve.wait_ge(bias_ready[h], count(0, 4, m0, jj))
                if u >= LOGIT_BUFS:
                    dve.wait_ge(tr_done, count(USE_T + u - 4 + 1, 9, m0, jj))
                else:
                    wait(dve, tr_done, count(USE_T - 9 + u + 4 + 1, 9, m0, jj))
                nc.vector.memset(gap[:, b:b + 1], 0.0)
                nc.vector.tensor_tensor_reduce(out=logit[b][:, 0:n], in0=ps_sc[u % 2][:, 0:n], in1=bias[h][:, i, 0:n],
                                               scale=-1.0, scalar=3e38, op0=ALU.add, op1=ALU.min,
                                               accum_out=nmax[:, b:b + 1]).then_inc(logit_ready, 1)

            def normalise(u, m0, jj):
                b, n = u % LOGIT_BUFS, (u % TT + 1) * P
                dve.wait_ge(exp_done, count(u + 1 - 8, 8, m0, jj))
                nc.vector.reciprocal(rrec[:, b:b + 1], rsum[:, b:b + 1]).then_inc(rec_done, 1)
                dve.wait_ge(rec_done, count(u + 1 - 8, 8, m0, jj))
                nc.vector.tensor_scalar(logit[b][:, 0:n], logit[b][:, 0:n], rrec[:, b:b + 1], None, ALU.mult
                                        ).then_inc(prob_ready, 1)

            def pt_rest(u, m0, jj):
                n, i = USE_T + 9 * m0 + u, u % TT
                dve.wait_ge(pt_hi_done, count(u + 1 - 8, 8, m0, jj))
                nc.vector.tensor_tensor(causal(pt_lo, i), ps_tr[n % TR_BANKS][:, 0:(i + 1) * P].rearrange("p (k c) -> p k c", c=P),
                                        causal(pt_hi, i), ALU.subtract).then_inc(tr_free[n % TR_BANKS], 1)

            def head_sum(h, m0, jj):
                dve.wait_ge(o_half_done, count(h - 1, 2, m0, jj))
                own = slice(h * DH, h * DH + DH)
                nc.vector.tensor_tensor(o_u[own, :], ps_o[own, :], o_half[own, :], ALU.add).then_inc(o_free, 1)

            def turn(m0, jj, project, attend):
                m = m0 + 2 * jj
                b = m0 % 2
                s = STEP_QKVZ + 4 * m0
                for g in range(GROUPS):
                    if attend and g - 1 in SCORE_AT:
                        normalise(SCORE_AT[g - 1], m0, jj)
                    if attend and g in SCORE_AT:
                        score_logits(SCORE_AT[g], m0, jj)
                    if attend and g in TRANSPOSE_AT:
                        pt_rest(TRANSPOSE_AT[g], m0, jj)
                    if g == 1 and attend:
                        dve.wait_ge(z_tanh_done, m)
                        nc.vector.scalar_tensor_tensor(z_silu[:], z_tanh[:], 1.0, ps_pj[(s - 1) % 2][:], ALU.add,
                                                       ALU.mult).then_inc(pj_free[(s - 1) % 2], 1)
                    if g in (5, 6) and project:
                        h = g - 5
                        dve.wait_ge(q_hi_done, count(h + 1, 2, m0, jj))
                        for r in range(2):
                            part = slice(h * DH, h * DH + DH)
                            last = nc.vector.scalar_tensor_tensor(
                                q_lo[b][h][r * DH:r * DH + DH, :], ps_pj[s % 2][part, :], DH ** -0.5,
                                q_hi[b][h][part, :], ALU.mult, ALU.subtract)
                        if h == 1:
                            last.then_inc(pj_free[s % 2], 1)
                    if g == 9 and project:
                        dve.wait_ge(k_hi_done, m + 1)
                        for h in range(2):
                            own, other = slice(h * DH, h * DH + DH), slice(DH - h * DH, 2 * DH - h * DH)
                            last = nc.vector.tensor_tensor(k_st[b][h][other, :], ps_pj[(s + 1) % 2][own, :],
                                                           k_st[b][h][own, :], ALU.subtract)
                        last.then_inc(pj_free[(s + 1) % 2], 1)
                    if attend and g in SUM_AT:
                        head_sum(SUM_AT[g], m0, jj)
                    if attend and g == GROUPS - 1:
                        dve.wait_ge(o_free, count(0, 2, m0, jj))
                        nc.vector.scalar_tensor_tensor(o_u[:], o_u[:], 0.5, z_silu[:], ALU.mult, ALU.mult
                                                       ).then_inc(u_ready, 1)
                    if g == GROUPS - 1 and project:
                        n = USE_V
                        dve.wait_ge(v_hi_done, m + 1)
                        dst = v_st[:].rearrange("p t (a b c) -> p t a b c", a=2, c=DH)
                        src = ps_tr[n % TR_BANKS][:].rearrange("p (t h c) -> p t h c", h=2, c=DH)
                        for h in range(2):
                            last = nc.vector.tensor_tensor(dst[:, :, h, 1 - h, :], src[:, :, h, :],
                                                           dst[:, :, h, h, :], ALU.subtract)
                        last.then_inc(tr_free[n % TR_BANKS], 1)
                    if attend and g == GROUPS - 1:
                        dve.wait_ge(act_hi_done, m + KT)
                        tile = bass.ds(m - 1, 1)
                        nc.vector.tensor_tensor(act_lo[1][:, tile, :], o_u[:].rearrange("p (o c) -> p o c", o=1),
                                                act_hi[1][:, tile, :], ALU.subtract).then_inc(act_ready, 1)

            turn(0, 0, True, False)
            turn(1, 0, True, True)
            with dve.Fori(0, (PAIRS - 2) // 2) as jj:
                turn(2, jj, True, True)
                turn(3, jj, True, True)
            turn(PAIRS, 0, False, True)

            chained = [0]

            def chain(ins):
                ins.then_inc(v_self, 1)
                chained[0] += 1
                return chained[0]

            def norm(n):
                dve.wait_ge(acc_hi_done, n + 1)
                nc.vector.tensor_tensor(acc_lo[:], acc[:], acc_hi[:], ALU.subtract).then_inc(acc_ready, 1)
                dve.wait_ge(root_done, n + 1)
                nc.vector.reciprocal(rs[:], rs_root[:]).then_inc(rs_ready, 1)
                dve.wait_ge(rs_ready, n + 1)

            for l in range(2):
                a_g, a_h = (act_hi[l], act_lo[l]), (act_hi[1 - l], act_lo[1 - l])
                dve.wait_ge(p_hi_done, l + 1)
                nc.vector.tensor_tensor(p_lo[:], p_in[:], p_hi[:], ALU.subtract).then_inc(p_ready, 1)
                norm(3 * l)
                if l == 0:
                    dve.wait_ge(res_loaded, 16)
                for m in range(KT + 1):
                    if m < KT and m % 2 == 1:
                        link = chain(nc.vector.tensor_tensor(t_a[1][:], yT[:, m, :], rs[:], ALU.mult))
                    if m > 0:
                        if m % 2 == 0:
                            dve.wait_ge(v_self, link)
                        else:
                            dve.wait_ge(y_scaled, KT // 2 * l + m // 2 + 1)
                        nc.vector.tensor_tensor(xT[:, m - 1, :], xT[:, m - 1, :], t_a[(m - 1) % 2][:], ALU.add
                                                ).then_inc(x_new, 1)
                        dve.wait_ge(act_hi_done, ACT_G[l] + m)
                        nc.vector.scalar_tensor_tensor(a_g[1][:, m - 1, :], xT[:, m - 1, :], g_pe[:, l, m - 1:m],
                                                       a_g[0][:, m - 1, :], ALU.mult, ALU.subtract
                                                       ).then_inc(act_ready, 1)
                norm(3 * l + 1)
                for m in range(KT):
                    s = STEP_GATE[l] + m
                    dve.wait_ge(pj_done, s + 1)
                    nc.vector.tensor_tensor(t_a[m % 2][:], ps_pj[s % 2][:], rs[:], ALU.mult
                                            ).then_inc(pj_free[s % 2], 1)
                    dve.wait_ge(g_tanh, KT * l + m + 1)
                    ple = pleT[:, m, :] if m < PLE_STEPS else ps_ple[m - PLE_STEPS][:]
                    link = chain(nc.vector.scalar_tensor_tensor(t_a[m % 2][:], t_b[m % 2][:], 1.0, ple,
                                                                ALU.add, ALU.mult))
                    dve.wait_ge(v_self, link)
                    nc.vector.scalar_tensor_tensor(xT[:, m, :], t_a[m % 2][:], 0.5, xT[:, m, :], ALU.mult, ALU.add
                                                   ).then_inc(x_new, 1)
                    if l == 0:
                        dve.wait_ge(act_hi_done, ACT_H[1] + m + 1)
                        nc.vector.scalar_tensor_tensor(a_h[1][:, m, :], xT[:, m, :], g_pre[:, 1, m:m + 1],
                                                       a_h[0][:, m, :], ALU.mult, ALU.subtract
                                                       ).then_inc(act_ready, 1)
                if l == 1:
                    continue
                norm(2)
                nc.vector.memset(cv_w[:, 0:TAPS - 1], 0.0).then_inc(cv_pad, 1)
                link = chain(nc.vector.tensor_tensor(rs2[:], rs[:], rs[:], ALU.mult))
                dve.wait_ge(v_self, link)
                dve.wait_ge(cv_pad, 1)
                dve.wait_ge(g_loaded[4], 16)
                with dve.Fori(0, KT) as m:
                    s = [STEP_CONV + j for j in range(4)]
                    bank = [ps_pj[i % 2] for i in s]
                    dve.wait_ge(pj_done, 4 * m + s[0] + 1)
                    nc.vector.tensor_tensor(cv_c[:], bank[0][:], rs2[:], ALU.mult).then_inc(pj_free[s[0] % 2], 1)
                    dve.wait_ge(pj_free[s[0] % 2], 2 * m + s[0] // 2 + 1)
                    dve.wait_ge(pj_done, 4 * m + s[1] + 1)
                    nc.vector.tensor_tensor(cv_w[:, TAPS - 1:TAPS - 1 + SEQ], bank[1][:], cv_c[:], ALU.mult
                                            ).then_inc(pj_free[s[1] % 2], 1)
                    dve.wait_ge(pj_free[s[1] % 2], 2 * m + s[1] // 2 + 1)
                    nc.vector.tensor_scalar(cv_y[0][:], cv_w[:, 2:2 + SEQ], taps[:, 2, bass.ds(m, 1)], None, ALU.mult
                                            ).then_inc(cv_self, 1)
                    dve.wait_ge(cv_self, 6 * m + 1)
                    nc.vector.scalar_tensor_tensor(cv_y[1][:], cv_w[:, 1:1 + SEQ], taps[:, 1, bass.ds(m, 1)],
                                                   cv_y[0][:], ALU.mult, ALU.add).then_inc(cv_self, 1)
                    dve.wait_ge(cv_self, 6 * m + 2)
                    nc.vector.scalar_tensor_tensor(cv_y[0][:], cv_w[:, 0:SEQ], taps[:, 0, bass.ds(m, 1)],
                                                   cv_y[1][:], ALU.mult, ALU.add).then_inc(cv_self, 1)
                    dve.wait_ge(cv_self, 6 * m + 3)
                    dve.wait_ge(pj_done, 4 * m + s[2] + 1)
                    nc.vector.tensor_tensor(cv_y[1][:], bank[2][:], cv_y[0][:], ALU.mult
                                            ).then_inc(pj_free[s[2] % 2], 1)
                    dve.wait_ge(pj_done, 4 * m + s[3] + 1)
                    nc.vector.tensor_tensor(cv_z[:], bank[3][:], rs[:], ALU.mult).then_inc(pj_free[s[3] % 2], 1)
                    dve.wait_ge(cz_tanh, m + 1)
                    nc.vector.scalar_tensor_tensor(cv_t[:], cv_t[:], 1.0, cv_z[:], ALU.add, ALU.mult
                                                   ).then_inc(cv_self, 1)
                    dve.wait_ge(cv_self, 6 * m + 4)
                    nc.vector.scalar_tensor_tensor(cv_t[:], cv_t[:], 0.5, rs[:], ALU.mult, ALU.mult
                                                   ).then_inc(cv_self, 1)
                    dve.wait_ge(cv_self, 6 * m + 5)
                    nc.vector.tensor_tensor(cv_z[:], cv_y[1][:], cv_t[:], ALU.mult).then_inc(cv_self, 1)
                    dve.wait_ge(act_hi_done, m + ACT_U[1] + 1)
                    tile = bass.ds(m, 1)
                    nc.vector.tensor_tensor(act_lo[0][:, tile, :], cv_z[:].rearrange("p (o c) -> p o c", o=1),
                                            act_hi[0][:, tile, :], ALU.subtract).then_inc(act_ready, 1)

        @block.tensor
        def _(pe):
            def products(bank, place, a, ks, first, last, w=None):
                for k in ks:
                    w_h = w_hi[place % RING][:, k, :] if w is None else w[k][0]
                    w_l = w_lo[place % RING][:, k, :] if w is None else w[k][1]
                    nc.tensor.matmul(bank[:], w_h, a[0][:, k, :], start=k == first, stop=False)
                    nc.tensor.matmul(bank[:], w_h, a[1][:, k, :], start=False, stop=False)
                    end = nc.tensor.matmul(bank[:], w_l, a[0][:, k, :], start=False, stop=k == last)
                return end

            act0, act1 = (act_hi[0], act_lo[0]), (act_hi[1], act_lo[1])

            def transposes(n, tiles, done=tr_done):
                for t, tile in enumerate(tiles):
                    last = nc.tensor.transpose(ps_tr[n % TR_BANKS][:, t * P:(t + 1) * P], tile, ident[:])
                last.then_inc(done, 1)

            pe.wait_ge(consts, 3)
            pe.wait_ge(x_norm, TT)
            for k in range(KT):
                if k >= TR_BANKS:
                    pe.wait_ge(act_ready, k - TR_BANKS + 1)
                transposes(k, [x_n[:, t, k * P:(k + 1) * P] for t in range(TT)], xn_done)
            pe.wait_ge(w_ready, SLOT_F + 1)
            for k in range(KT):
                pe.wait_ge(act_ready, k + 1)
                end = products(ps_pj[0], 0, act0, [k], 0, KT - 1)
            end.then_inc(pj_done, 1)

            def turn(m0, jj, project, attend):
                b = m0 % 2
                for g in range(GROUPS):
                    j = g // 4
                    s = STEP_QKVZ + 4 * m0 + j
                    if attend and g in TRANSPOSE_AT:
                        u = TRANSPOSE_AT[g]
                        pe.wait_ge(prob_ready, count(u + 1 - 8, 8, m0, jj))
                        wait(pe, tr_free[(USE_T + u) % TR_BANKS], tr_uses(USE_T + u, m0, jj))
                        transposes(USE_T + u, [logit[u % LOGIT_BUFS][:, k * P:(k + 1) * P] for k in range(u % TT + 1)])
                    if g == V_AT and project:
                        sv = STEP_QKVZ + 4 * m0 + 2
                        pe.wait_ge(pj_free[sv % 2], halved(STEP_QKVZ + 2, 4, m0, jj) + 1)
                        wait(pe, tr_free[USE_V % TR_BANKS], tr_uses(USE_V, m0, jj))
                        transposes(USE_V, [vT[:, t * P:(t + 1) * P] for t in range(TT)])
                    if attend and g in SCORE_AT:
                        u = SCORE_AT[g]
                        h, i = u // TT, u % TT
                        if g == 0:
                            sk = STEP_QKVZ + 4 * (m0 - 1) + 1
                            pe.wait_ge(pj_free[sk % 2], halved(STEP_QKVZ - 3 + 2, 4, m0, jj))
                        wait(pe, logit_ready, count(u - 8 - 1, 8, m0, jj))
                        queries, keys = slice(i * P, (i + 1) * P), slice(0, (i + 1) * P)
                        nc.tensor.matmul(ps_sc[u % 2][:, keys], q_hi[1 - b][h][:, queries], k_st[1 - b][h][:, keys],
                                         start=True, stop=False)
                        nc.tensor.matmul(ps_sc[u % 2][:, keys], q_lo[1 - b][h][:, queries], k_st[1 - b][h][:, keys],
                                         start=False, stop=True).then_inc(sc_done, 1)
                    if project:
                        if g % 4 == 0:
                            pe.wait_ge(w_ready, count(SLOT_QKVZ + j + 1, 4, m0, jj))
                            wait(pe, pj_free[s % 2], halved(STEP_QKVZ + j, 4, m0, jj))
                        k = 2 * (g % 4)
                        end = products(ps_pj[s % 2], s, act0, [k, k + 1], 0, KT - 1)
                        if g % 4 == 3:
                            end.then_inc(pj_done, 1)
                    elif g < 2 * (KT - 1):
                        j, k = g // (KT - 1), g % (KT - 1)
                        s = STEP_OUT[0] + j
                        if k == 0:
                            pe.wait_ge(w_ready, SLOT_OUT[0] + j + 1)
                            pe.wait_ge(pj_free[s % 2], s // 2)
                        if j == 0:
                            pe.wait_ge(act_ready, ACT_U[0] + k + 1)
                        products(ps_pj[s % 2], SLOT_OUT[0] + j, act1, [k], 0, KT - 1)
                    if attend and g in PV_AT:
                        h = PV_AT[g]
                        n = USE_T + 4 * h + 3
                        pe.wait_ge(tr_free[n % TR_BANKS], tr_uses(n, m0, jj) + 1)
                        wait(pe, o_free, count(h - 2, 2, m0, jj))
                        for k in range(TT):
                            cols = slice(k * PT_STEP + k * P, k * PT_STEP + SEQ)
                            v = v_st[:, k, h * P:(h + 1) * P]
                            nc.tensor.matmul(ps_o[:, k * P:SEQ], v, pt_hi[:, cols], start=k == 0, stop=False)
                            last = nc.tensor.matmul(ps_o[:, k * P:SEQ], v, pt_lo[:, cols], start=False,
                                                    stop=k == TT - 1)
                        last.then_inc(pv_done, 1)

            turn(0, 0, True, False)
            turn(1, 0, True, True)
            with pe.Fori(0, (PAIRS - 2) // 2) as jj:
                turn(2, jj, True, True)
                turn(3, jj, True, True)
            turn(PAIRS, 0, False, True)

            def step(s, slot, a, tiles, from_k=0):
                pe.wait_ge(w_ready, slot + 1)
                pe.wait_ge(pj_free[s % 2], s // 2)
                for k in range(from_k, KT):
                    pe.wait_ge(act_ready, tiles + k + 1)
                    end = products(ps_pj[s % 2], slot, a, [k], 0, KT - 1)
                end.then_inc(pj_done, 1)

            def two_steps(s, slot, a, tiles, norm_at, n):
                for j in range(2):
                    pe.wait_ge(w_ready, slot + j + 1)
                    pe.wait_ge(pj_free[(s + j) % 2], (s + j) // 2)
                for k in range(KT):
                    if k == norm_at:
                        norm(n)
                    pe.wait_ge(act_ready, tiles + k + 1)
                    for j in range(2):
                        end = products(ps_pj[(s + j) % 2], slot + j, a, [k], 0, KT - 1)
                        if k == KT - 1:
                            end.then_inc(pj_done, 1)

            def norm(n):
                pe.wait_ge(acc_ready, n + 1)
                pe.wait_ge(mean_ready, 2)
                wait(pe, root_done, n)
                nc.tensor.matmul(ps_o[:], mean_w[:], acc_hi[:], start=True, stop=False)
                nc.tensor.matmul(ps_o[:], mean_w[:], acc_lo[:], start=False, stop=True).then_inc(st_done, 1)

            for l in range(2):
                a_u, a_g = (act1, act0) if l == 0 else (act0, act1)
                if l == 1:
                    two_steps(STEP_OUT[l], SLOT_OUT[l], a_u, ACT_U[l], None, None)
                for m in range(2 * l, KT):
                    step(STEP_OUT[l] + m, SLOT_OUT[l] + m, a_u, ACT_U[l], KT - 1 if l == 0 and m < 2 else 0)
                pe.wait_ge(p_ready, l + 1)
                pe.wait_ge(w_ready, SLOT_PLE[l] + PLE_KT)
                w_ple = lambda m: [(w_hi[(SLOT_PLE[l] + k) % RING][:, m, :], w_lo[(SLOT_PLE[l] + k) % RING][:, m, :])
                                   for k in range(PLE_KT)]
                for m in range(PLE_STEPS, KT):
                    products(ps_ple[m - PLE_STEPS], 0, (p_hi, p_lo), range(PLE_KT), 0, PLE_KT - 1, w_ple(m))
                    if m == PLE_STEPS + 1:
                        norm(3 * l)
                for m in range(PLE_STEPS):
                    s = STEP_PLE[l] + m
                    pe.wait_ge(pj_free[s % 2], s // 2)
                    end = products(ps_pj[s % 2], 0, (p_hi, p_lo), range(PLE_KT), 0, PLE_KT - 1, w_ple(m))
                    end.then_inc(pj_done, 1)
                two_steps(STEP_GATE[l], SLOT_GATE[l], a_g, ACT_G[l], KT - 1, 3 * l + 1)
                for m in range(2, KT):
                    step(STEP_GATE[l] + m, SLOT_GATE[l] + m, a_g, ACT_G[l])
                if l == 0:
                    two_steps(STEP_CONV, SLOT_CONV, act1, ACT_H[1], KT - 3, 2)

                    def conv_steps(m, js):
                        for j in js:
                            s, slot = STEP_CONV + j, SLOT_CONV + j
                            pe.wait_ge(w_ready, 4 * m + slot + 1)
                            pe.wait_ge(pj_free[s % 2], 2 * m + s // 2)
                            end = products(ps_pj[s % 2], slot, act1, range(KT), 0, KT - 1)
                            end.then_inc(pj_done, 1)

                    conv_steps(0, [2, 3])
                    with pe.Fori(1, KT) as m:
                        conv_steps(m, range(4))


def slots(w):
    n = w.shape[1] // P
    return w.reshape(KT, P, n, P).transpose(2, 1, 0, 3).reshape(n, P, D)


def weight_stream(attn_w_in, attn_w_out, conv_w_in, conv_w_out, pe_w_gate, pe_w_proj):
    f = np.zeros((D, P), attn_w_in.dtype)
    f[:, :HEADS] = attn_w_in[0][:, 4 * D:]
    qkvz = slots(attn_w_in[0][:, :4 * D]).reshape(4, PAIRS, P, D).transpose(1, 0, 2, 3).reshape(4 * PAIRS, P, D)
    bchz = slots(conv_w_in[0]).reshape(4, KT, P, D)
    chbz = bchz[[1, 2, 0, 3]].transpose(1, 0, 2, 3).reshape(4 * KT, P, D)
    tails = [[slots(w[0]), pe_w_proj[i].reshape(PLE_KT, P, D), slots(pe_w_gate[i])]
             for i, w in enumerate((attn_w_out, conv_w_out))]
    return np.concatenate([slots(f), qkvz, *tails[0], chbz, *tails[1]])


def kernel(**inputs):
    import concourse.bacc as bacc
    from concourse.bass_utils import run_bass_kernel_spmd

    a = {name: np.asarray(value) for name, value in inputs.items()}
    by_feature = lambda v: v.reshape(-1, KT, P).transpose(2, 0, 1)
    arrays = {
        "in_x": a["x"][0],
        "in_xT": a["x"][0].T.reshape(KT, P, SEQ),
        "in_pT": a["p"][:, 0].transpose(0, 2, 1).reshape(2, PLE_KT, P, SEQ).transpose(0, 2, 1, 3),
        "in_weights": weight_stream(a["attn_w_in"], a["attn_w_out"], a["conv_w_in"], a["conv_w_out"],
                                    a["pe_w_gate"], a["pe_w_proj"]),
        "in_b_f": a["attn_b_f"].reshape(HEADS, 1),
        "in_norm_pre": by_feature(a["norm_pre"]),
        "in_norm_post": by_feature(a["norm_post"]),
        "in_pe_norm": by_feature(a["pe_norm"]),
        "in_taps": by_feature(a["conv_kernel"][0]),
    }
    arrays = {name: np.ascontiguousarray(value) for name, value in arrays.items()}
    nc = bacc.Bacc("TRN2", target_bir_lowering=False, num_devices=1)
    args = [nc.dram_tensor(name, v.shape, mybir.dt.from_np(v.dtype), kind="ExternalInput").ap()
            for name, v in arrays.items()]
    out = nc.dram_tensor("out_0", (KT, P, SEQ), F32, kind="ExternalOutput").ap()
    trunk(nc, *args, out)
    result = run_bass_kernel_spmd(nc, [arrays], core_ids=[0])
    return result.results[0]["out_0"].reshape(D, SEQ).T.reshape(1, SEQ, D)
```

```python
from contextlib import ExitStack

import numpy as np
import concourse.bass as bass
from concourse import mybir

F32 = mybir.dt.float32
F32R = mybir.dt.float32r
ALU = mybir.AluOpType
ACT = mybir.ActivationFunctionType

P = 128
SEQ = 512
D = 1024
KT = D // P
TT = SEQ // P
HEADS = 16
DH = D // HEADS
PAIRS = HEADS // 2
PLE = 256
PLE_KT = PLE // P
TAPS = 3
EPS = 1e-6
MASKED = -1e30
RING = 4
RAW = 2
LOGIT_BUFS = 4
PT_STEP = (TT - 1) * P
PLE_STEPS = KT // 2

WIDE = 2
STEP_QKVZ = 0
TAIL_STEPS = 2 * (KT - 1) + PLE_STEPS
STEP_OUT = [STEP_QKVZ + 4 * PAIRS, STEP_QKVZ + 4 * PAIRS + TAIL_STEPS + 4 * KT]
STEP_PLE = [s + KT - 1 for s in STEP_OUT]
STEP_GATE = [s + PLE_STEPS for s in STEP_PLE]
STEP_CONV = STEP_OUT[0] + TAIL_STEPS
SLOT_QKVZ = 0
SLOT_OUT = [SLOT_QKVZ + 4 * PAIRS, SLOT_QKVZ + 4 * PAIRS + 6 * KT]
SLOT_GATE = [s + KT for s in SLOT_OUT]
SLOT_CONV = SLOT_GATE[0] + KT
SLOTS = SLOT_GATE[1] + KT
PLE_AFTER = [6, 8]
F_PART = 32
TR_BANKS = 3
POOL_TILES = [1, 4]
USE_V = 0
USE_T = -8
ACT_H = [0, 3 * KT]
ACT_U = [KT, 4 * KT]
ACT_G = [2 * KT, 5 * KT]
SCORE_AT = {0: 0, 1: 1, 2: 2, 3: 3, 6: 4, 7: 5, 8: 6, 9: 7}
TRANSPOSE_AT = {3: 0, 4: 1, 5: 2, 6: 3, 9: 4, 10: 5, 11: 6, 12: 7}
PV_AT = {8: 0, 13: 1}
SUM_AT = {9: 0, 14: 1}
WEIGHTS_AT = 2
V_AT = 14
GROUPS = 16
PLE_COPY_AT = {0: [1], 1: [2, 3]}
P_AT = 4
NORM_AFTER = KT - 3
BEHIND = 3


def wait(eng, sem, count):
    if not isinstance(count, int) or count > 0:
        eng.wait_ge(sem, count)


def stream(slot):
    return slot + sum(slot > s + after for s in SLOT_OUT for after in PLE_AFTER)


def ple_stream(l, k):
    return stream(SLOT_OUT[l] + PLE_AFTER[k]) + 1


def tile_step(first, m):
    return first + m - (m > WIDE)


def trunk(nc, xT_in, pT_in, weights, f_in, b_f_in, pre_in, post_in, pe_in, taps_in, outT):
    negc_dram = nc.dram_tensor("negc_scratch", [HEADS, SEQ], F32).ap()

    ctx = ExitStack()
    with ctx:
        def sb(name, shape, dt=F32, at=ctx):
            return at.enter_context(nc.sbuf_tensor(name, shape, dt))

        def sem(name):
            return ctx.enter_context(nc.semaphore(name))

        xT = sb("xT", [P, KT, SEQ])
        act_hi = [sb(f"act{i}_hi", [P, KT, SEQ], F32R) for i in range(2)]
        act_lo = [sb(f"act{i}_lo", [P, KT, SEQ], F32R) for i in range(2)]
        w_raw = [sb(f"w_raw{i}", [P, KT, P]) for i in range(RAW)]
        w_hi = [sb(f"w_hi{i}", [P, KT, P], F32R) for i in range(RING)]
        w_lo = [sb(f"w_lo{i}", [P, KT, P], F32R) for i in range(RING)]
        ident = sb("ident", [P, P])
        future = sb("future", [P, P])
        mean_f = sb("mean_f", [P, P])
        mean_w = sb("mean_w", [P, P], F32R)
        g_pre = sb("g_pre", [P, 2, KT])
        g_post = sb("g_post", [P, 2, KT])
        g_pe = sb("g_pe", [P, 2, KT])
        taps = sb("taps", [P, TAPS, KT])
        rs = sb("rs", [P, SEQ])
        b_f = sb("b_f", [HEADS, 1])
        gap = sb("gap", [P, LOGIT_BUFS])
        nmax = sb("nmax", [P, LOGIT_BUFS])
        rsum = sb("rsum", [P, LOGIT_BUFS])
        rrec = sb("rrec", [P, LOGIT_BUFS])
        norms = ExitStack()
        sq = [sb(f"sq{i}", [P, SEQ], at=norms) for i in range(2)]
        acc = sb("acc", [P, SEQ], at=norms)
        acc_hi = sb("acc_hi", [P, SEQ], F32R, norms)
        acc_lo = sb("acc_lo", [P, SEQ], F32R, norms)
        root = sb("root", [P, TT], at=norms)
        r_tok = sb("r_tok", [P, TT], at=norms)
        r_row = sb("r_row", [P, TT, P], at=norms)
        f_part = ExitStack()
        f_raw = sb("f_raw", [P, KT, F_PART], at=f_part)
        f_w = sb("f_w", [P, KT, 2 * F_PART], F32R, f_part)
        ones_f = sb("ones_f", [HEADS, SEQ], at=f_part)
        f_half = sb("f_half", [HEADS, SEQ], at=f_part)
        f_x = [sb(f"f_x{i}", [HEADS, SEQ], at=f_part) for i in range(2)]
        f_abs = sb("f_abs", [HEADS, SEQ], at=f_part)
        f_ln = sb("f_ln", [HEADS, SEQ], at=f_part)
        f_negc = f_abs
        f_part.close()
        late = ExitStack()
        conv = ExitStack()
        cv_c = sb("cv_c", [P, SEQ], at=conv)
        cv_w = sb("cv_w", [P, TAPS - 1 + SEQ], at=conv)
        cv_y = [sb(f"cv_y{i}", [P, SEQ], at=conv) for i in range(2)]
        cv_z = sb("cv_z", [P, SEQ], at=conv)
        cv_t = sb("cv_t", [P, SEQ], at=conv)
        conv.close()
        yT = sb("yT", [P, KT, SEQ], at=late)
        pleT = sb("pleT", [P, PLE_STEPS, SEQ], at=late)
        w_ple_hi = sb("w_ple_hi", [P, PLE_KT, D], F32R, late)
        w_ple_lo = sb("w_ple_lo", [P, PLE_KT, D], F32R, late)
        p_in = sb("p_in", [P, PLE_KT, SEQ], at=late)
        p_hi = sb("p_hi", [P, PLE_KT, SEQ], F32R, late)
        p_lo = sb("p_lo", [P, PLE_KT, SEQ], F32R, late)
        rs2 = sb("rs2", [P, SEQ], at=late)
        g_raw = [sb(f"g_raw{i}", [P, SEQ], at=late) for i in range(2)]
        t_a = [sb(f"t_a{i}", [P, SEQ], at=late) for i in range(2)]
        t_b = [sb(f"t_b{i}", [P, SEQ], at=late) for i in range(2)]
        late.close()
        norms.close()

        attn = ExitStack()
        logit = [sb(f"logit{i}", [P, SEQ], at=attn) for i in range(LOGIT_BUFS)]
        pt_hi = sb("pt_hi", [P, TT * PT_STEP + PT_STEP], F32R, attn)
        pt_lo = sb("pt_lo", [P, TT * PT_STEP + PT_STEP], F32R, attn)
        o_half = sb("o_half", [P, SEQ], at=attn)
        o_u = sb("o_u", [P, SEQ], at=attn)
        v_st = sb("v_st", [P, TT, 4 * DH], F32R, attn)
        scaled = [sb(f"scaled{i}", [P, SEQ], at=attn) for i in range(2)]
        z_tanh = sb("z_tanh", [P, SEQ], at=attn)
        z_silu = sb("z_silu", [P, SEQ], at=attn)
        q_hi = [[sb(f"q_hi{b}{h}", [P, SEQ], F32R, attn) for h in range(2)] for b in range(2)]
        q_lo = [[sb(f"q_lo{b}{h}", [P, SEQ], F32R, attn) for h in range(2)] for b in range(2)]
        k_st = [[sb(f"k_st{b}{h}", [P, SEQ], F32R, attn) for h in range(2)] for b in range(2)]
        bias = [sb(f"bias{h}", [P, TT, SEQ], at=attn) for h in range(2)]
        attn.close()
        ps_pj = [ctx.enter_context(nc.psum_tensor(f"ps_pj{i}", [P, SEQ], F32)) for i in range(2)]
        ps_sc = [ctx.enter_context(nc.psum_tensor(f"ps_sc{i}", [P, SEQ], F32)) for i in range(2)]
        ps_tr = [ctx.enter_context(nc.psum_tensor(f"ps_tr{i}", [P, SEQ], F32)) for i in range(TR_BANKS)]
        ps_o = ctx.enter_context(nc.psum_tensor("ps_o", [P, SEQ], F32))
        ps_wide = ps_tr[2]
        ps_ple = [ps_sc[0], ps_sc[1], ps_tr[0], ps_tr[1]]

        x_loaded = [sem(f"x_loaded{k}") for k in range(KT)]
        f_loaded = sem("f_loaded")
        g_loaded = [sem(f"g_loaded{i}") for i in range(5)]
        p_loaded = sem("p_loaded")
        w_loaded = [sem(f"w_loaded{i}") for i in range(RAW)]
        w_hi_done = sem("w_hi_done")
        w_ready = sem("w_ready")
        pj_done = sem("pj_done")
        pj_free = [sem(f"pj_free{i}") for i in range(2)]
        f_hi_done = sem("f_hi_done")
        f_ready = sem("f_ready")
        f_done = sem("f_done")
        f_half_done = sem("f_half_done")
        f_self = sem("f_self")
        tr_done = sem("tr_done")
        tr_free = [sem(f"tr_free{i}") for i in range(TR_BANKS)]
        consts = sem("consts")
        mean_ready = sem("mean_ready")
        x_sq = sem("x_sq")
        x_acc = sem("x_acc")
        act_hi_done = sem("act_hi_done")
        act_ready = sem("act_ready")
        f_chain = sem("f_chain")
        f_act = sem("f_act")
        negc_stored = sem("negc_stored")
        bias_loaded = [sem(f"bias_loaded{h}") for h in range(2)]
        bias_ready = [sem(f"bias_ready{h}") for h in range(2)]
        q_hi_done = sem("q_hi_done")
        q_lo_done = sem("q_lo_done")
        k_hi_done = sem("k_hi_done")
        qk_ready = sem("qk_ready")
        v_hi_done = sem("v_hi_done")
        z_tanh_done = sem("z_tanh_done")
        sc_done = sem("sc_done")
        logit_ready = sem("logit_ready")
        exp_done = sem("exp_done")
        rec_done = sem("rec_done")
        prob_ready = sem("prob_ready")
        pt_hi_done = sem("pt_hi_done")
        pv_done = sem("pv_done")
        o_half_done = sem("o_half_done")
        o_free = sem("o_free")
        u_ready = sem("u_ready")
        p_hi_done = sem("p_hi_done")
        p_ready = sem("p_ready")
        sq_ready = sem("sq_ready")
        acc_done = sem("acc_done")
        acc_hi_done = sem("acc_hi_done")
        acc_ready = sem("acc_ready")
        st_done = sem("st_done")
        root_done = sem("root_done")
        r_tok_done = sem("r_tok_done")
        r_row_done = sem("r_row_done")
        spread_done = sem("spread_done")
        rs_ready = sem("rs_ready")
        wide_done = sem("wide_done")
        g_copied = sem("g_copied")
        g_scaled = sem("g_scaled")
        x_new = sem("x_new")
        y_scaled = sem("y_scaled")
        v_self = sem("v_self")
        g_tanh = sem("g_tanh")
        cv_pad = sem("cv_pad")
        cv_self = sem("cv_self")
        cz_tanh = sem("cz_tanh")
        stored = sem("stored")

        block = ctx.enter_context(nc.Block())

        def count(c, per, m0, jj):
            return c + per * m0 + 2 * per * jj

        def halved(c, per, m0, jj):
            return (c + per * m0) // 2 + per * jj

        def tr_uses(c, m0, jj):
            return c // TR_BANKS + 9 // TR_BANKS * (m0 + 2 * jj)

        def last_step(slot):
            for l in range(2):
                for first_slot, first in ((SLOT_OUT[l], STEP_OUT[l]), (SLOT_GATE[l], STEP_GATE[l])):
                    m = slot - first_slot
                    if 0 <= m < KT:
                        return tile_step(first, m - (m == WIDE))
            return slot + (TAIL_STEPS - 2 * KT) * (slot >= SLOT_CONV)

        def parts(l, m):
            n = 2 if l == 1 and m == KT - 1 else 1
            return [slice(i * SEQ // n, (i + 1) * SEQ // n) for i in range(n)]

        def causal(pt, i):
            part = pt[:, i * P:i * P + PT_STEP * (i + 1)]
            return part.rearrange("p (k c) -> p k c", c=PT_STEP)[:, :, 0:P]

        @block.sync
        def _(sp):
            def load_slot(slot, place):
                wait(sp, w_ready, slot - RAW + 1)
                src = weights[bass.ds(slot, 1), :, :].rearrange("o p (k c) -> p (o k) c", c=P)
                sp.dma_start(w_raw[place % RAW][:], src).then_inc(w_loaded[place % RAW], 16)

            def load_bias(a, h):
                wait(sp, logit_ready, 8 * a - 8 + 4 * h + 4)
                for i in range(TT):
                    n = (i + 1) * P
                    row = negc_dram[bass.ds(2 * a + h, 1), 0:n]
                    sp.dma_start(bias[h][:, i, 0:n], row.to_broadcast([P, n])).then_inc(bias_loaded[h], 16)

            for k in range(KT):
                sp.dma_start(xT[:, k, :], xT_in[k]).then_inc(x_loaded[k], 16)
                if k == 0:
                    sp.dma_start(g_pre[:], pre_in).then_inc(g_loaded[0], 16)
                    sp.dma_start(f_raw[:], f_in).then_inc(f_loaded, 16)
                if k == 1 or k == 3:
                    load_slot(k // 2, k // 2)
            sp.dma_start(b_f[:], b_f_in).then_inc(g_loaded[1], 16)
            for slot in range(2, 6):
                load_slot(slot, slot)
            sp.dma_start(g_post[:], post_in).then_inc(g_loaded[2], 16)
            sp.dma_start(g_pe[:], pe_in).then_inc(g_loaded[3], 16)
            sp.dma_start(taps[:], taps_in).then_inc(g_loaded[4], 16)
            sp.wait_ge(f_chain, 3)
            sp.dma_start(negc_dram, f_negc[:]).then_inc(negc_stored, 16)
            sp.wait_ge(negc_stored, 16)

            def turn(m):
                load_bias(m, 0)
                load_slot(6 + 4 * m, 6)
                load_slot(7 + 4 * m, 7)
                load_bias(m, 1)
                load_slot(8 + 4 * m, 8)
                load_slot(9 + 4 * m, 9)

            turn(0)
            with sp.Fori(1, PAIRS) as m:
                turn(m)
            after = stream(SLOT_CONV) + RAW
            for slot in range(6 + 4 * PAIRS, after):
                load_slot(slot, slot)
                if slot == 7 + 4 * PAIRS:
                    sp.wait_ge(act_ready, ACT_U[0] + KT)
                    sp.dma_start(p_in[:], pT_in[0]).then_inc(p_loaded, 16)
            with sp.Fori(0, KT) as m:
                for j in range(4):
                    load_slot(4 * m + after + j, after + j)
            sp.wait_ge(p_ready, 1)
            sp.dma_start(p_in[:], pT_in[1]).then_inc(p_loaded, 16)
            for slot in range(after + 4 * KT, stream(SLOTS)):
                load_slot(slot, slot)
            for m in range(KT):
                for i, tokens in enumerate(parts(1, m)):
                    sp.wait_ge(x_new, 3 * KT + m + i + 1)
                    sp.dma_start(outT[m, :, tokens], xT[:, m, tokens]).then_inc(stored, 16)
            sp.wait_ge(stored, 16 * (KT + 1))

        @block.gpsimd
        def _(pool):
            nc.gpsimd.memset(ident[:], 0.0).then_inc(consts, 1)
            pool.wait_ge(consts, 1)
            nc.gpsimd.affine_select(out=ident[:], in_=ident[:], compare_op=ALU.not_equal, fill=1.0, base=0,
                                    pattern=[[-1, P]], channel_multiplier=1).then_inc(consts, 1)
            nc.gpsimd.memset(mean_f[:], 1.0 / D).then_inc(consts, 1)
            nc.gpsimd.memset(future[:], 0.0).then_inc(consts, 1)
            pool.wait_ge(consts, 4)
            nc.gpsimd.affine_select(out=future[:], in_=future[:], compare_op=ALU.is_ge, fill=MASKED, base=0,
                                    pattern=[[-1, P]], channel_multiplier=1).then_inc(consts, 1)
            pool.wait_ge(consts, 5)

            def weight_lo(slot, place):
                pool.wait_ge(w_hi_done, slot + stream(place) - place + 1)
                if place in [slot + 3 for slot in SLOT_GATE]:
                    pool.wait_ge(w_ready, stream(place))
                nc.gpsimd.tensor_tensor(w_lo[place % RING][:], w_raw[stream(place) % RAW][:], w_hi[place % RING][:],
                                        ALU.subtract).then_inc(w_ready, 1)

            def mask(a, h):
                pool.wait_ge(bias_loaded[h], 64 * a + 64)
                for i in range(TT):
                    diagonal = bias[h][:, i, i * P:(i + 1) * P]
                    nc.gpsimd.tensor_tensor(diagonal, diagonal, future[:], ALU.add).then_inc(bias_ready[h], 1)

            def turn(m):
                weight_lo(3 + 4 * m, 3)
                weight_lo(4 + 4 * m, 4)
                mask(m, 0)
                weight_lo(5 + 4 * m, 5)
                weight_lo(6 + 4 * m, 6)
                mask(m, 1)

            pool.wait_ge(f_hi_done, 1)
            nc.gpsimd.tensor_tensor(f_w[:, :, F_PART:2 * F_PART], f_raw[:], f_w[:, :, 0:F_PART], ALU.subtract
                                    ).then_inc(f_ready, 1)
            for slot in range(3):
                weight_lo(slot, slot)
            with pool.Fori(0, PAIRS) as m:
                turn(m)
            weight_lo(SLOT_OUT[0] + 3, SLOT_OUT[0] + 3)

            def add_square(n):
                if n % KT > 0:
                    pool.wait_ge(sq_ready, n - n // KT)
                    pool.wait_ge(acc_done, n)
                    nc.gpsimd.tensor_tensor(acc[:], acc[:], sq[n % 2][:], ALU.add).then_inc(acc_done, 1)

            for l in range(2):
                pool.wait_ge(rs_ready, 3 * l + 2)
                for m in range(KT):
                    for i, tile in enumerate(POOL_TILES):
                        if m == 2 * i:
                            nc.gpsimd.tensor_tensor(t_b[i][:], yT[:, tile, :], rs[:], ALU.mult).then_inc(y_scaled, 1)
                    add_square(3 * KT * l + KT + m)
                    if m == 4:
                        weight_lo(SLOT_GATE[l] + 3, SLOT_GATE[l] + 3)
                for m in range(KT):
                    for slot in ([4, 5] if m == 0 else [m + 5]):
                        if slot < KT + 3 * (l == 0):
                            weight_lo(SLOT_GATE[l] + slot, SLOT_GATE[l] + slot)
                if l == 0:
                    with pool.Fori(0, KT) as m:
                        for j in range(4):
                            weight_lo(4 * m + SLOT_CONV + 3 + j, SLOT_CONV + 3 + j)

        @block.scalar
        def _(act):
            def weight_hi(slot, place):
                position = stream(place)
                act.wait_ge(w_loaded[position % RAW], 16 * (position // RAW + 1) + (16 // RAW) * (slot - place))
                if place >= RING:
                    act.wait_ge(pj_done, last_step(place - RING) + 1 + (slot - place))
                nc.scalar.copy(w_hi[place % RING][:], w_raw[position % RAW][:]).then_inc(w_hi_done, 1)

            def ple_weight_hi(l, k):
                position = ple_stream(l, k)
                act.wait_ge(w_loaded[position % RAW], 16 * (position // RAW + 1))
                nc.scalar.copy(w_ple_hi[:, k], w_raw[position % RAW][:].rearrange("p k c -> p (k c)")
                               ).then_inc(w_hi_done, 1)

            act.wait_ge(f_loaded, 16)
            nc.scalar.copy(f_w[:, :, 0:F_PART], f_raw[:]).then_inc(f_hi_done, 1)
            act.wait_ge(g_loaded[0], 16)
            for k in range(KT):
                act.wait_ge(x_loaded[k], 16)
                nc.scalar.activation(act_hi[0][:, k, :], xT[:, k, :], ACT.Copy, scale=g_pre[:, 0, k:k + 1]
                                     ).then_inc(act_hi_done, 1)
                wait(act, x_acc, k - 1)
                nc.scalar.activation(sq[k % 2][:], xT[:, k, :], ACT.Square).then_inc(x_sq, 1)
                if k % 2 == 1 and k < 4:
                    weight_hi(k // 2, k // 2)

            def norm_sum(n):
                if n == 0:
                    act.wait_ge(x_acc, KT)
                else:
                    act.wait_ge(acc_done, KT * n)
                wait(act, st_done, n)
                nc.scalar.copy(acc_hi[:], acc[:]).then_inc(acc_hi_done, 1)

            def norm_root(n):
                act.wait_ge(st_done, n + 1)
                nc.scalar.activation(root[:], ps_o[:, 0:2 * TT:2], ACT.Sqrt, bias=EPS).then_inc(root_done, 1)

            def norm_spread(n):
                act.wait_ge(spread_done, n + 1)
                nc.scalar.copy(rs[:], ps_o[:]).then_inc(rs_ready, 1)

            norm_sum(0)
            act.wait_ge(f_done, 1)
            nc.scalar.copy(f_half[:], ps_sc[0][F_PART:F_PART + HEADS, :]).then_inc(f_half_done, 1)
            norm_root(0)
            weight_hi(2, 2)
            norm_spread(0)

            def score_exp(u, m0, jj):
                act.wait_ge(logit_ready, count(u + 1 - 8, 8, m0, jj))
                b, n = u % LOGIT_BUFS, (u % TT + 1) * P
                nc.scalar.activation(logit[b][:, 0:n], logit[b][:, 0:n], ACT.Exp, scale=-1.0, bias=nmax[:, b:b + 1],
                                     accum_out=rsum[:, b:b + 1]).then_inc(exp_done, 1)

            def pt_round(u, m0, jj):
                n = USE_T + 9 * m0 + u
                act.wait_ge(tr_done, count(USE_T + u + 1, 9, m0, jj))
                if u % TT == 0:
                    wait(act, pv_done, count(u // TT - 2, 2, m0, jj))
                i = u % TT
                nc.scalar.copy(causal(pt_hi, i), ps_tr[n % TR_BANKS][:, 0:(i + 1) * P].rearrange("p (k c) -> p k c", c=P)
                               ).then_inc(pt_hi_done, 1)

            def head_half(h, m0, jj):
                act.wait_ge(pv_done, count(h - 1, 2, m0, jj))
                wait(act, o_free, count(h + 1 - 4, 2, m0, jj))
                own, other = slice(h * DH, h * DH + DH), slice(DH - h * DH, 2 * DH - h * DH)
                nc.scalar.copy(o_half[own, :], ps_o[other, :]).then_inc(o_half_done, 1)

            def turn(m0, jj, project, attend):
                m = m0 + 2 * jj
                b = m0 % 2
                s = STEP_QKVZ + 4 * m0
                for g in range(GROUPS):
                    if attend and g in TRANSPOSE_AT:
                        pt_round(TRANSPOSE_AT[g], m0, jj)
                    if attend and g in SCORE_AT:
                        score_exp(SCORE_AT[g], m0, jj)
                    if g == 1 and attend:
                        act.wait_ge(pj_free[(s - 1) % 2], halved(STEP_QKVZ - 1, 4, m0, jj) + 1)
                        nc.scalar.activation(z_tanh[:], scaled[1][:], ACT.Tanh, scale=0.5
                                             ).then_inc(z_tanh_done, 1)
                    if g in (4, 5) and project:
                        h = g - 4
                        act.wait_ge(pj_free[s % 2], halved(STEP_QKVZ, 4, m0, jj) + 1)
                        for r in range(2):
                            last = nc.scalar.copy(q_hi[b][h][r * DH:r * DH + DH, :], scaled[0][h * DH:h * DH + DH, :])
                        last.then_inc(q_hi_done, 1)
                    if g == 8 and project:
                        act.wait_ge(pj_free[(s + 1) % 2], halved(STEP_QKVZ + 1, 4, m0, jj) + 1)
                        for h in range(2):
                            own = slice(h * DH, h * DH + DH)
                            last = nc.scalar.copy(k_st[b][h][own, :], scaled[1][own, :])
                        last.then_inc(k_hi_done, 1)
                    if g == WEIGHTS_AT and not project:
                        weight_hi(SLOT_OUT[0] + 3, SLOT_OUT[0] + 3)
                    if g % 4 == WEIGHTS_AT and project:
                        weight_hi(count(3 + g // 4, 4, m0, jj), 3 + 4 * m0 + g // 4)
                    if not attend and g == 3:
                        act.wait_ge(f_chain, 1)
                        nc.scalar.activation(f_ln[:], f_abs[:], ACT.Exp, scale=-1.0).then_inc(f_act, 1)
                        act.wait_ge(f_act, 1)
                        nc.scalar.activation(f_ln[:], f_ln[:], ACT.Ln, bias=1.0).then_inc(f_act, 1)
                    if attend and g in SUM_AT:
                        head_half(SUM_AT[g], m0, jj)
                    if g == V_AT and project:
                        n = USE_V
                        act.wait_ge(tr_done, count(USE_V + 1, 9, m0, jj))
                        wait(act, pv_done, count(0, 2, m0, jj))
                        dst = v_st[:].rearrange("p t (a b c) -> p t a b c", a=2, c=DH)
                        src = ps_tr[n % TR_BANKS][:].rearrange("p (t h c) -> p t h c", h=2, c=DH)
                        for h in range(2):
                            last = nc.scalar.copy(dst[:, :, h, h, :], src[:, :, h, :])
                        last.then_inc(v_hi_done, 1)
                    if attend and g == GROUPS - 1:
                        act.wait_ge(u_ready, m)
                        nc.scalar.copy(act_hi[1][:, bass.ds(m - 1, 1), :], o_u[:].rearrange("p (o c) -> p o c", o=1)
                                       ).then_inc(act_hi_done, 1)

            turn(0, 0, True, False)
            turn(1, 0, True, True)
            with act.Fori(0, (PAIRS - 2) // 2) as jj:
                turn(2, jj, True, True)
                turn(3, jj, True, True)
            turn(PAIRS, 0, False, True)

            def square(n, src):
                if n % KT == 0:
                    act.wait_ge(acc_ready, n // KT + 1)
                    nc.scalar.activation(acc[:], src, ACT.Square).then_inc(acc_done, 1)
                else:
                    wait(act, acc_done, n - 1)
                    nc.scalar.activation(sq[n % 2][:], src, ACT.Square).then_inc(sq_ready, 1)

            for l in range(2):
                a_g, a_h = act_hi[l], act_hi[1 - l]
                if l == 1:
                    weight_hi(SLOT_OUT[l] + 3, SLOT_OUT[l] + 3)
                for m in range(KT):
                    s = tile_step(STEP_OUT[l], m)
                    if m == WIDE:
                        act.wait_ge(wide_done, 2 * l + 1)
                        bank = ps_wide
                    else:
                        act.wait_ge(pj_done, s + 1)
                        bank = ps_pj[s % 2]
                    square(3 * KT * l + m, bank[:])
                    if m == 0:
                        act.wait_ge(g_loaded[2], 16)
                    last = nc.scalar.activation(yT[:, m, :], bank[:], ACT.Copy, scale=g_post[:, l, m:m + 1])
                    if m != WIDE:
                        last.then_inc(pj_free[s % 2], 1)
                    if m < KT - 1:
                        weight_hi(SLOT_OUT[l] + m + 4, SLOT_OUT[l] + m + 4)
                    if m + 4 in PLE_AFTER:
                        ple_weight_hi(l, PLE_AFTER.index(m + 4))
                    if m == P_AT:
                        act.wait_ge(p_loaded, 16 * l + 16)
                        nc.scalar.copy(p_hi[:], p_in[:]).then_inc(p_hi_done, 1)
                norm_sum(3 * l + 1)
                norm_root(3 * l + 1)
                norm_spread(3 * l + 1)
                act.wait_ge(g_loaded[3], 16)

                def ple_copy(m):
                    s = STEP_PLE[l] + m
                    act.wait_ge(pj_done, s + 1)
                    nc.scalar.copy(pleT[:, m, :], ps_pj[s % 2][:]).then_inc(pj_free[s % 2], 1)

                ple_copy(0)
                for m in range(KT):
                    act.wait_ge(x_new, 2 * KT * l + m + 1)
                    nc.scalar.activation(a_g[:, m, :], xT[:, m, :], ACT.Copy, scale=g_pe[:, l, m:m + 1]
                                         ).then_inc(act_hi_done, 1)
                    for tile in PLE_COPY_AT.get(m, []):
                        ple_copy(tile)
                    square(3 * KT * l + KT + m, xT[:, m, :])
                    if m == 4:
                        weight_hi(SLOT_GATE[l] + 3, SLOT_GATE[l] + 3)

                def gate_copy(m):
                    if l == 1 and m == KT - 1:
                        return
                    wait(act, g_scaled, KT * l + m - 1)
                    if m == WIDE:
                        act.wait_ge(wide_done, 2 * l + 2)
                        nc.scalar.copy(g_raw[m % 2][:], ps_wide[:]).then_inc(g_copied, 1)
                    else:
                        s = tile_step(STEP_GATE[l], m)
                        act.wait_ge(pj_done, s + 1)
                        nc.scalar.copy(g_raw[m % 2][:], ps_pj[s % 2][:]).then_inc(pj_free[s % 2], 1)

                def gate_weight(m):
                    if m < KT + 3 * (l == 0):
                        weight_hi(SLOT_GATE[l] + m, SLOT_GATE[l] + m)

                norm_sum(3 * l + 2)
                gate_copy(0)
                gate_copy(1)
                norm_root(3 * l + 2)
                norm_spread(3 * l + 2)
                gate_weight(4)
                def gate_next(m):
                    if l == 0 and m >= 0:
                        act.wait_ge(x_new, KT + m + 1)
                        nc.scalar.activation(a_h[:, m, :], xT[:, m, :], ACT.Copy, scale=g_pre[:, 1, m:m + 1]
                                             ).then_inc(act_hi_done, 1)
                        square(2 * KT + m, xT[:, m, :])

                for m in range(KT):
                    if m >= 2 and m != WIDE + 1:
                        gate_copy(m)
                    if m == 1:
                        gate_weight(m + 4)
                    for i, tokens in enumerate(parts(l, m)):
                        act.wait_ge(g_scaled, KT * l + m + i + 1)
                        nc.scalar.activation(t_b[m % 2][:, tokens], t_a[m % 2][:, tokens], ACT.Tanh, scale=0.5
                                             ).then_inc(g_tanh, 1)
                    if m == WIDE:
                        gate_copy(m + 1)
                    gate_next(m - 1)
                    if m > 1:
                        gate_weight(m + 4)
                gate_next(KT - 1)
                if l == 0:
                    norm_sum(3)
                    norm_root(3)
                    norm_spread(3)
                    with act.Fori(0, KT) as m:
                        for j in range(4):
                            slot = SLOT_CONV + 3 + j
                            weight_hi(4 * m + slot, slot)
                        sz = STEP_CONV + 3
                        act.wait_ge(pj_free[sz % 2], sz // 2 + 1 + 2 * m)
                        nc.scalar.activation(cv_t[:], cv_z[:], ACT.Tanh, scale=0.5).then_inc(cz_tanh, 1)
                        act.wait_ge(cv_self, 6 * m + 6)
                        nc.scalar.copy(act_hi[0][:, bass.ds(m, 1), :], cv_z[:].rearrange("p (o c) -> p o c", o=1)
                                       ).then_inc(act_hi_done, 1)

        @block.vector
        def _(dve):
            def norm(n, meanwhile=None):
                dve.wait_ge(acc_hi_done, n + 1)
                nc.vector.tensor_tensor(acc_lo[:], acc[:], acc_hi[:], ALU.subtract).then_inc(acc_ready, 1)
                if meanwhile:
                    meanwhile()
                dve.wait_ge(root_done, n + 1)
                nc.vector.reciprocal(r_tok[:], root[:]).then_inc(r_tok_done, 1)
                dve.wait_ge(r_tok_done, n + 1)
                wait(dve, spread_done, n)
                nc.vector.tensor_copy(r_row[:], r_tok[:].rearrange("p (t o) -> p t o", o=1).to_broadcast([P, TT, P])
                                      ).then_inc(r_row_done, 1)
                dve.wait_ge(rs_ready, n + 1)

            dve.wait_ge(consts, 3)
            nc.vector.tensor_copy(mean_w[:], mean_f[:]).then_inc(mean_ready, 1)
            nc.vector.memset(ones_f[:], 1.0).then_inc(mean_ready, 1)
            for k in range(KT):
                dve.wait_ge(act_hi_done, k + 1)
                nc.vector.scalar_tensor_tensor(act_lo[0][:, k, :], xT[:, k, :], g_pre[:, 0, k:k + 1],
                                               act_hi[0][:, k, :], ALU.mult, ALU.subtract
                                               ).then_inc(act_ready, 1)
                dve.wait_ge(x_sq, k + 1)
                if k == 0:
                    nc.vector.tensor_copy(acc[:], sq[0][:]).then_inc(x_acc, 1)
                else:
                    dve.wait_ge(x_acc, k)
                    nc.vector.tensor_tensor(acc[:], acc[:], sq[k % 2][:], ALU.add).then_inc(x_acc, 1)

            def f_parts():
                dve.wait_ge(f_half_done, 1)
                nc.vector.tensor_tensor(f_x[0][:], ps_sc[0][0:HEADS, :], f_half[:], ALU.add).then_inc(f_self, 1)

            norm(0, f_parts)

            def f_logits():
                dve.wait_ge(f_self, 1)
                nc.vector.tensor_tensor(f_x[1][:], f_x[0][:], rs[0:HEADS, :], ALU.mult).then_inc(f_self, 1)
                dve.wait_ge(g_loaded[1], 16)
                dve.wait_ge(f_self, 2)
                nc.vector.tensor_scalar(f_x[0][:], f_x[1][:], b_f[:], None, ALU.add).then_inc(f_self, 1)
                dve.wait_ge(f_self, 3)
                nc.vector.scalar_tensor_tensor(f_abs[:], f_x[0][:], -1.0, f_x[0][:], ALU.mult, ALU.max
                                               ).then_inc(f_chain, 1)

            def f_sums():
                dve.wait_ge(f_act, 2)
                nc.vector.scalar_tensor_tensor(f_x[1][:], f_x[0][:], 0.0, f_ln[:], ALU.min, ALU.subtract
                                               ).then_inc(f_chain, 1)
                dve.wait_ge(mean_ready, 2)
                dve.wait_ge(f_chain, 2)
                nc.vector.tensor_tensor_scan(f_negc[:], ones_f[:], f_x[1][:], 0.0, ALU.mult, ALU.subtract
                                             ).then_inc(f_chain, 1)

            def score_logits(u, m0, jj):
                h, i, b, n = u // TT, u % TT, u % LOGIT_BUFS, (u % TT + 1) * P
                dve.wait_ge(sc_done, count(u + 1 - 8, 8, m0, jj))
                if i == 0:
                    dve.wait_ge(bias_ready[h], count(0, 4, m0, jj))
                if u >= LOGIT_BUFS:
                    dve.wait_ge(tr_done, count(USE_T + u - 4 + 1, 9, m0, jj))
                else:
                    wait(dve, tr_done, count(USE_T - 9 + u + 4 + 1, 9, m0, jj))
                nc.vector.memset(gap[:, b:b + 1], 0.0)
                nc.vector.tensor_tensor_reduce(out=logit[b][:, 0:n], in0=ps_sc[u % 2][:, 0:n], in1=bias[h][:, i, 0:n],
                                               scale=-1.0, scalar=3e38, op0=ALU.add, op1=ALU.min,
                                               accum_out=nmax[:, b:b + 1]).then_inc(logit_ready, 1)

            def normalise(u, m0, jj):
                b, n = u % LOGIT_BUFS, (u % TT + 1) * P
                dve.wait_ge(exp_done, count(u + 1 - 8, 8, m0, jj))
                nc.vector.reciprocal(rrec[:, b:b + 1], rsum[:, b:b + 1]).then_inc(rec_done, 1)
                dve.wait_ge(rec_done, count(u + 1 - 8, 8, m0, jj))
                nc.vector.tensor_scalar(logit[b][:, 0:n], logit[b][:, 0:n], rrec[:, b:b + 1], None, ALU.mult
                                        ).then_inc(prob_ready, 1)

            def pt_rest(u, m0, jj):
                n, i = USE_T + 9 * m0 + u, u % TT
                dve.wait_ge(pt_hi_done, count(u + 1 - 8, 8, m0, jj))
                nc.vector.tensor_tensor(causal(pt_lo, i), ps_tr[n % TR_BANKS][:, 0:(i + 1) * P].rearrange("p (k c) -> p k c", c=P),
                                        causal(pt_hi, i), ALU.subtract).then_inc(tr_free[n % TR_BANKS], 1)

            def head_sum(h, m0, jj):
                dve.wait_ge(o_half_done, count(h - 1, 2, m0, jj))
                own = slice(h * DH, h * DH + DH)
                nc.vector.tensor_tensor(o_u[own, :], ps_o[own, :], o_half[own, :], ALU.add).then_inc(o_free, 1)

            def turn(m0, jj, project, attend):
                m = m0 + 2 * jj
                b = m0 % 2
                s = STEP_QKVZ + 4 * m0

                def scale(j):
                    bank = (s + j) % 2
                    dve.wait_ge(pj_done, count(STEP_QKVZ + j + 1, 4, m0, jj))
                    nc.vector.scalar_tensor_tensor(scaled[j % 2][:], ps_pj[bank][:], DH ** -0.5 if j == 0 else 1.0,
                                                   rs[:], ALU.mult, ALU.mult).then_inc(pj_free[bank], 1)

                for g in range(GROUPS):
                    if g == 0 and attend:
                        scale(-1)
                    if g == 4 and project:
                        scale(0)
                    if g == 4 and not attend:
                        f_logits()
                        scale(1)
                        f_sums()
                    if g == 8 and project and attend:
                        scale(1)
                    if g == 12 and project:
                        dve.wait_ge(q_lo_done, m + 1)
                        scale(2)
                    if attend and g - 1 in SCORE_AT:
                        normalise(SCORE_AT[g - 1], m0, jj)
                    if attend and g in SCORE_AT:
                        score_logits(SCORE_AT[g], m0, jj)
                    if attend and g in TRANSPOSE_AT:
                        pt_rest(TRANSPOSE_AT[g], m0, jj)
                    if g == 2 and attend:
                        dve.wait_ge(z_tanh_done, m)
                        nc.vector.scalar_tensor_tensor(z_silu[:], z_tanh[:], 1.0, scaled[1][:], ALU.add, ALU.mult)
                    if g in (5, 6) and project:
                        h = g - 5
                        dve.wait_ge(q_hi_done, count(h + 1, 2, m0, jj))
                        for r in range(2):
                            part = slice(h * DH, h * DH + DH)
                            last = nc.vector.tensor_tensor(q_lo[b][h][r * DH:r * DH + DH, :], scaled[0][part, :],
                                                           q_hi[b][h][part, :], ALU.subtract)
                        if h == 1:
                            last.then_inc(q_lo_done, 1)
                    if g == 9 and project:
                        dve.wait_ge(k_hi_done, m + 1)
                        for h in range(2):
                            own, other = slice(h * DH, h * DH + DH), slice(DH - h * DH, 2 * DH - h * DH)
                            last = nc.vector.tensor_tensor(k_st[b][h][other, :], scaled[1][own, :],
                                                           k_st[b][h][own, :], ALU.subtract)
                        last.then_inc(qk_ready, 1)
                    if attend and g in SUM_AT:
                        head_sum(SUM_AT[g], m0, jj)
                    if attend and g == GROUPS - 1:
                        dve.wait_ge(o_free, count(0, 2, m0, jj))
                        nc.vector.scalar_tensor_tensor(o_u[:], o_u[:], 0.5, z_silu[:], ALU.mult, ALU.mult
                                                       ).then_inc(u_ready, 1)
                    if g == GROUPS - 1 and project:
                        n = USE_V
                        dve.wait_ge(v_hi_done, m + 1)
                        dst = v_st[:].rearrange("p t (a b c) -> p t a b c", a=2, c=DH)
                        src = ps_tr[n % TR_BANKS][:].rearrange("p (t h c) -> p t h c", h=2, c=DH)
                        for h in range(2):
                            last = nc.vector.tensor_tensor(dst[:, :, h, 1 - h, :], src[:, :, h, :],
                                                           dst[:, :, h, h, :], ALU.subtract)
                        last.then_inc(tr_free[n % TR_BANKS], 1)
                    if attend and g == GROUPS - 1:
                        dve.wait_ge(act_hi_done, m + KT)
                        tile = bass.ds(m - 1, 1)
                        nc.vector.tensor_tensor(act_lo[1][:, tile, :], o_u[:].rearrange("p (o c) -> p o c", o=1),
                                                act_hi[1][:, tile, :], ALU.subtract).then_inc(act_ready, 1)

            turn(0, 0, True, False)
            turn(1, 0, True, True)
            with dve.Fori(0, (PAIRS - 2) // 2) as jj:
                turn(2, jj, True, True)
                turn(3, jj, True, True)
            turn(PAIRS, 0, False, True)

            chained = [0]

            def add_square(n):
                if n % KT > 0:
                    dve.wait_ge(sq_ready, n - n // KT)
                    dve.wait_ge(acc_done, n)
                    nc.vector.tensor_tensor(acc[:], acc[:], sq[n % 2][:], ALU.add).then_inc(acc_done, 1)

            def chain(ins):
                ins.then_inc(v_self, 1)
                chained[0] += 1
                return chained[0]

            for l in range(2):
                a_g, a_h = (act_hi[l], act_lo[l]), (act_hi[1 - l], act_lo[1 - l])

                def weight_lo(position, lo, hi):
                    dve.wait_ge(w_hi_done, position + 1)
                    dve.wait_ge(w_ready, position)
                    raw = w_raw[position % RAW][:].rearrange("p k c -> p (k c)")
                    nc.vector.tensor_tensor(lo, raw, hi, ALU.subtract).then_inc(w_ready, 1)

                def slot_lo(slot):
                    lo, hi = (w[slot % RING][:].rearrange("p k c -> p (k c)") for w in (w_lo, w_hi))
                    weight_lo(stream(slot), lo, hi)

                if l == 1:
                    slot_lo(SLOT_OUT[l] + 3)
                for m in range(KT):
                    add_square(3 * KT * l + m)
                    if m < KT - 1:
                        slot_lo(SLOT_OUT[l] + m + 4)
                    if m + 4 in PLE_AFTER:
                        k = PLE_AFTER.index(m + 4)
                        weight_lo(ple_stream(l, k), w_ple_lo[:, k], w_ple_hi[:, k])
                    if m == P_AT:
                        dve.wait_ge(p_hi_done, l + 1)
                        nc.vector.tensor_tensor(p_lo[:], p_in[:], p_hi[:], ALU.subtract).then_inc(p_ready, 1)
                norm(3 * l + 1)
                links = {}
                for m in range(-1, KT + 1):
                    if 0 <= m < KT:
                        if m in POOL_TILES:
                            i = POOL_TILES.index(m)
                            dve.wait_ge(y_scaled, len(POOL_TILES) * l + i + 1)
                            branch = t_b[i]
                        else:
                            dve.wait_ge(v_self, links[m])
                            branch = t_a[m % 2]
                        nc.vector.tensor_tensor(xT[:, m, :], xT[:, m, :], branch[:], ALU.add).then_inc(x_new, 1)
                    if m > 0:
                        dve.wait_ge(act_hi_done, ACT_G[l] + m)
                        nc.vector.scalar_tensor_tensor(a_g[1][:, m - 1, :], xT[:, m - 1, :], g_pe[:, l, m - 1:m],
                                                       a_g[0][:, m - 1, :], ALU.mult, ALU.subtract
                                                       ).then_inc(act_ready, 1)
                    if m + 1 < KT and m + 1 not in POOL_TILES:
                        links[m + 1] = chain(nc.vector.tensor_tensor(t_a[(m + 1) % 2][:], yT[:, m + 1, :], rs[:],
                                                                     ALU.mult))
                norm(3 * l + 2)

                def gate_rest(m):
                    if l == 0 and m >= 0:
                        dve.wait_ge(act_hi_done, ACT_H[1] + m + 1)
                        nc.vector.scalar_tensor_tensor(a_h[1][:, m, :], xT[:, m, :], g_pre[:, 1, m:m + 1],
                                                       a_h[0][:, m, :], ALU.mult, ALU.subtract
                                                       ).then_inc(act_ready, 1)
                        add_square(2 * KT + m)

                def gate_scale(m):
                    if l == 1 and m == KT - 1:
                        for i, tokens in enumerate(parts(l, m)):
                            s = tile_step(STEP_GATE[l], m)
                            dve.wait_ge(pj_done, s + i + 1)
                            nc.vector.tensor_tensor(t_a[m % 2][:, tokens], ps_pj[(s + i) % 2][:, tokens], rs[:, tokens],
                                                    ALU.mult).then_inc(g_scaled, 1)
                        return
                    if m == WIDE:
                        dve.wait_ge(g_copied, l + 1)
                    else:
                        s = tile_step(STEP_GATE[l], m)
                        dve.wait_ge(pj_free[s % 2], s // 2 + 1)
                    nc.vector.tensor_tensor(t_a[m % 2][:], g_raw[m % 2][:], rs[:], ALU.mult).then_inc(g_scaled, 1)

                gate_scale(0)
                for m in range(KT):
                    if m == 0:
                        gate_scale(1)
                    elif m > 1:
                        gate_scale(m)
                    ple = pleT[:, m, :] if m < PLE_STEPS else ps_ple[m - PLE_STEPS][:]
                    for i, tokens in enumerate(parts(l, m)):
                        dve.wait_ge(g_tanh, KT * l + m + i + 1)
                        link = chain(nc.vector.scalar_tensor_tensor(t_a[m % 2][:, tokens], t_b[m % 2][:, tokens], 1.0,
                                                                    ple[:, tokens], ALU.add, ALU.mult))
                        dve.wait_ge(v_self, link)
                        nc.vector.scalar_tensor_tensor(xT[:, m, tokens], t_a[m % 2][:, tokens], 0.5, xT[:, m, tokens],
                                                       ALU.mult, ALU.add).then_inc(x_new, 1)
                    gate_rest(m - 1)
                gate_rest(KT - 1)
                if l == 1:
                    continue
                nc.vector.memset(cv_w[:, 0:TAPS - 1], 0.0).then_inc(cv_pad, 1)
                norm(3)
                link = chain(nc.vector.tensor_tensor(rs2[:], rs[:], rs[:], ALU.mult))
                dve.wait_ge(v_self, link)
                dve.wait_ge(cv_pad, 1)
                dve.wait_ge(g_loaded[4], 16)
                with dve.Fori(0, KT) as m:
                    s = [STEP_CONV + j for j in range(4)]
                    bank = [ps_pj[i % 2] for i in s]
                    dve.wait_ge(pj_done, 4 * m + s[0] + 1)
                    nc.vector.tensor_tensor(cv_c[:], bank[0][:], rs2[:], ALU.mult).then_inc(pj_free[s[0] % 2], 1)
                    dve.wait_ge(pj_free[s[0] % 2], 2 * m + s[0] // 2 + 1)
                    dve.wait_ge(pj_done, 4 * m + s[1] + 1)
                    nc.vector.tensor_tensor(cv_w[:, TAPS - 1:TAPS - 1 + SEQ], bank[1][:], cv_c[:], ALU.mult
                                            ).then_inc(pj_free[s[1] % 2], 1)
                    dve.wait_ge(pj_free[s[1] % 2], 2 * m + s[1] // 2 + 1)
                    nc.vector.tensor_scalar(cv_y[0][:], cv_w[:, 2:2 + SEQ], taps[:, 2, bass.ds(m, 1)], None, ALU.mult
                                            ).then_inc(cv_self, 1)
                    dve.wait_ge(cv_self, 6 * m + 1)
                    nc.vector.scalar_tensor_tensor(cv_y[1][:], cv_w[:, 1:1 + SEQ], taps[:, 1, bass.ds(m, 1)],
                                                   cv_y[0][:], ALU.mult, ALU.add).then_inc(cv_self, 1)
                    dve.wait_ge(cv_self, 6 * m + 2)
                    nc.vector.scalar_tensor_tensor(cv_y[0][:], cv_w[:, 0:SEQ], taps[:, 0, bass.ds(m, 1)],
                                                   cv_y[1][:], ALU.mult, ALU.add).then_inc(cv_self, 1)
                    dve.wait_ge(cv_self, 6 * m + 3)
                    dve.wait_ge(pj_done, 4 * m + s[2] + 1)
                    nc.vector.tensor_tensor(cv_y[1][:], bank[2][:], cv_y[0][:], ALU.mult
                                            ).then_inc(pj_free[s[2] % 2], 1)
                    dve.wait_ge(pj_done, 4 * m + s[3] + 1)
                    nc.vector.tensor_tensor(cv_z[:], bank[3][:], rs[:], ALU.mult).then_inc(pj_free[s[3] % 2], 1)
                    dve.wait_ge(cz_tanh, m + 1)
                    nc.vector.scalar_tensor_tensor(cv_t[:], cv_t[:], 1.0, cv_z[:], ALU.add, ALU.mult
                                                   ).then_inc(cv_self, 1)
                    dve.wait_ge(cv_self, 6 * m + 4)
                    nc.vector.scalar_tensor_tensor(cv_t[:], cv_t[:], 0.5, rs[:], ALU.mult, ALU.mult
                                                   ).then_inc(cv_self, 1)
                    dve.wait_ge(cv_self, 6 * m + 5)
                    nc.vector.tensor_tensor(cv_z[:], cv_y[1][:], cv_t[:], ALU.mult).then_inc(cv_self, 1)
                    dve.wait_ge(act_hi_done, m + ACT_U[1] + 1)
                    tile = bass.ds(m, 1)
                    nc.vector.tensor_tensor(act_lo[0][:, tile, :], cv_z[:].rearrange("p (o c) -> p o c", o=1),
                                            act_hi[0][:, tile, :], ALU.subtract).then_inc(act_ready, 1)

        @block.tensor
        def _(pe):
            def products(bank, place, a, ks, first, last, w=None, tokens=slice(0, SEQ)):
                for k in ks:
                    w_h = w_hi[place % RING][:, k, :] if w is None else w[k][0]
                    w_l = w_lo[place % RING][:, k, :] if w is None else w[k][1]
                    out = bank[:, tokens]
                    nc.tensor.matmul(out, w_h, a[0][:, k, tokens], start=k == first, stop=False)
                    nc.tensor.matmul(out, w_h, a[1][:, k, tokens], start=False, stop=False)
                    end = nc.tensor.matmul(out, w_l, a[0][:, k, tokens], start=False, stop=k == last)
                return end

            act0, act1 = (act_hi[0], act_lo[0]), (act_hi[1], act_lo[1])

            def transposes(n, tiles):
                for t, tile in enumerate(tiles):
                    last = nc.tensor.transpose(ps_tr[n % TR_BANKS][:, t * P:(t + 1) * P], tile, ident[:])
                last.then_inc(tr_done, 1)

            def norm_sum(n):
                pe.wait_ge(acc_ready, n + 1)
                pe.wait_ge(mean_ready, 2)
                wait(pe, rs_ready, n)
                for t in range(TT):
                    tokens, column = slice(t * P, (t + 1) * P), ps_o[:, 2 * t:2 * t + 2]
                    nc.tensor.matmul(column, acc_hi[:, tokens], mean_w[:, 0:2], start=True, stop=False)
                    last = nc.tensor.matmul(column, acc_lo[:, tokens], mean_w[:, 0:2], start=False, stop=True)
                last.then_inc(st_done, 1)

            def norm_spread(n):
                pe.wait_ge(r_row_done, n + 1)
                for t in range(TT):
                    last = nc.tensor.transpose(ps_o[:, t * P:(t + 1) * P], r_row[:, t, :], ident[:])
                last.then_inc(spread_done, 1)

            pe.wait_ge(f_ready, 1)
            for k in range(KT + BEHIND):
                if k < KT:
                    pe.wait_ge(act_ready, k + 1)
                    nc.tensor.matmul(ps_sc[0][0:2 * F_PART, :], f_w[:, k, :], act_hi[0][:, k, :], start=k == 0,
                                     stop=False)
                    end = nc.tensor.matmul(ps_sc[0][0:2 * F_PART, :], f_w[:, k, :], act_lo[0][:, k, :], start=False,
                                           stop=k == KT - 1)
                    if k == KT - 1:
                        end.then_inc(f_done, 1)
                if k == KT + BEHIND - 1:
                    norm_sum(0)
                if k >= BEHIND:
                    if k == BEHIND:
                        pe.wait_ge(w_ready, SLOT_QKVZ + 1)
                    end = products(ps_pj[STEP_QKVZ % 2], SLOT_QKVZ, act0, [k - BEHIND], 0, KT - 1)
            end.then_inc(pj_done, 1)
            pe.wait_ge(w_ready, SLOT_QKVZ + 2)
            for k in range(KT):
                if k == 1:
                    norm_spread(0)
                end = products(ps_pj[(STEP_QKVZ + 1) % 2], SLOT_QKVZ + 1, act0, [k], 0, KT - 1)
            end.then_inc(pj_done, 1)

            def turn(m0, jj, project, attend):
                b = m0 % 2
                for g in range(GROUPS):
                    j = g // 4
                    s = STEP_QKVZ + 4 * m0 + j
                    if attend and g in TRANSPOSE_AT:
                        u = TRANSPOSE_AT[g]
                        pe.wait_ge(prob_ready, count(u + 1 - 8, 8, m0, jj))
                        wait(pe, tr_free[(USE_T + u) % TR_BANKS], tr_uses(USE_T + u, m0, jj))
                        transposes(USE_T + u, [logit[u % LOGIT_BUFS][:, k * P:(k + 1) * P] for k in range(u % TT + 1)])
                    if g == V_AT and project:
                        sv = STEP_QKVZ + 4 * m0 + 2
                        pe.wait_ge(pj_free[sv % 2], halved(STEP_QKVZ + 2, 4, m0, jj) + 1)
                        wait(pe, tr_free[USE_V % TR_BANKS], tr_uses(USE_V, m0, jj))
                        transposes(USE_V, [scaled[0][:, t * P:(t + 1) * P] for t in range(TT)])
                    if attend and g in SCORE_AT:
                        u = SCORE_AT[g]
                        h, i = u // TT, u % TT
                        if g == 0:
                            pe.wait_ge(qk_ready, count(0, 1, m0, jj))
                        if m0 == 1 and g == 0:
                            pe.wait_ge(f_chain, 1)
                        wait(pe, logit_ready, count(u - 8 - 1, 8, m0, jj))
                        queries, keys = slice(i * P, (i + 1) * P), slice(0, (i + 1) * P)
                        nc.tensor.matmul(ps_sc[u % 2][:, keys], q_hi[1 - b][h][:, queries], k_st[1 - b][h][:, keys],
                                         start=True, stop=False)
                        nc.tensor.matmul(ps_sc[u % 2][:, keys], q_lo[1 - b][h][:, queries], k_st[1 - b][h][:, keys],
                                         start=False, stop=True).then_inc(sc_done, 1)
                    if project and (m0 > 0 or j >= 2):
                        if g % 4 == 0:
                            pe.wait_ge(w_ready, count(SLOT_QKVZ + j + 1, 4, m0, jj))
                            wait(pe, pj_free[s % 2], halved(STEP_QKVZ + j, 4, m0, jj))
                        k = 2 * (g % 4)
                        end = products(ps_pj[s % 2], s, act0, [k, k + 1], 0, KT - 1)
                        if g % 4 == 3:
                            end.then_inc(pj_done, 1)
                    elif not project and g < 2 * (KT - 1):
                        j, k = g // (KT - 1), g % (KT - 1)
                        s = STEP_OUT[0] + j
                        if k == 0:
                            pe.wait_ge(w_ready, SLOT_OUT[0] + j + 1)
                            pe.wait_ge(pj_free[s % 2], s // 2)
                        if j == 0:
                            pe.wait_ge(act_ready, ACT_U[0] + k + 1)
                        products(ps_pj[s % 2], SLOT_OUT[0] + j, act1, [k], 0, KT - 1)
                    if attend and g in PV_AT:
                        h = PV_AT[g]
                        n = USE_T + 4 * h + 3
                        pe.wait_ge(tr_free[n % TR_BANKS], tr_uses(n, m0, jj) + 1)
                        wait(pe, o_free, count(h - 2, 2, m0, jj))
                        for k in range(TT):
                            cols = slice(k * PT_STEP + k * P, k * PT_STEP + SEQ)
                            v = v_st[:, k, h * P:(h + 1) * P]
                            nc.tensor.matmul(ps_o[:, k * P:SEQ], v, pt_hi[:, cols], start=k == 0, stop=False)
                            last = nc.tensor.matmul(ps_o[:, k * P:SEQ], v, pt_lo[:, cols], start=False,
                                                    stop=k == TT - 1)
                        last.then_inc(pv_done, 1)

            turn(0, 0, True, False)
            turn(1, 0, True, True)
            with pe.Fori(0, (PAIRS - 2) // 2) as jj:
                turn(2, jj, True, True)
                turn(3, jj, True, True)
            turn(PAIRS, 0, False, True)

            def weights_ready(slot, more=0):
                pe.wait_ge(w_ready, stream(slot) + 1 + more)

            def step(s, slot, a, tiles, tokens_in_turn=(slice(0, SEQ),), between={}):
                weights_ready(slot)
                for i, tokens in enumerate(tokens_in_turn):
                    bank = (s + i) % 2
                    pe.wait_ge(pj_free[bank], (s + i) // 2)
                    for k in range(KT):
                        if k in between:
                            between[k]()
                        pe.wait_ge(act_ready, tiles + k + 1)
                        end = products(ps_pj[bank], slot, a, [k], 0, KT - 1, tokens=tokens)
                    end.then_inc(pj_done, 1)

            def side_by_side(s, slot, a, tiles, wide=False, between={}, from_k=0):
                for k in range(from_k, KT):
                    pe.wait_ge(act_ready, tiles + k + 1)
                    for j in range(2):
                        if j == 1 and k in between:
                            between[k]()
                        if k == 0:
                            weights_ready(slot + j)
                            pe.wait_ge(pj_free[(s + j) % 2], (s + j) // 2)
                        end = products(ps_pj[(s + j) % 2], slot + j, a, [k], 0, KT - 1)
                        if k == KT - 1:
                            end.then_inc(pj_done, 1)
                    if wide:
                        if k == 0:
                            weights_ready(slot + WIDE)
                        end = products(ps_wide, slot + WIDE, a, [k], 0, KT - 1)
                        if k == KT - 1:
                            end.then_inc(wide_done, 1)

            for l in range(2):
                a_u, a_g = (act1, act0) if l == 0 else (act0, act1)
                if l == 0:
                    weights_ready(SLOT_OUT[l] + WIDE)
                    products(ps_wide, SLOT_OUT[l] + WIDE, a_u, range(KT - 1), 0, KT - 1)
                side_by_side(STEP_OUT[l], SLOT_OUT[l], a_u, ACT_U[l], True, from_k=(KT - 1) * (1 - l))
                for m in range(WIDE + 1, KT):
                    step(tile_step(STEP_OUT[l], m), SLOT_OUT[l] + m, a_u, ACT_U[l])
                pe.wait_ge(p_ready, l + 1)
                pe.wait_ge(w_ready, ple_stream(l, PLE_KT - 1) + 1)

                def ple_tile(bank, m):
                    w = [(w_ple_hi[:, k, m * P:(m + 1) * P], w_ple_lo[:, k, m * P:(m + 1) * P])
                         for k in range(PLE_KT)]
                    return products(bank, 0, (p_hi, p_lo), range(PLE_KT), 0, PLE_KT - 1, w)

                for m in range(PLE_STEPS, KT):
                    ple_tile(ps_ple[m - PLE_STEPS], m)
                    if m == NORM_AFTER:
                        norm_sum(3 * l + 1)
                    if m == NORM_AFTER + 1:
                        norm_spread(3 * l + 1)
                for m in range(PLE_STEPS):
                    s = STEP_PLE[l] + m
                    pe.wait_ge(pj_free[s % 2], s // 2)
                    ple_tile(ps_pj[s % 2], m).then_inc(pj_done, 1)
                side_by_side(STEP_GATE[l], SLOT_GATE[l], a_g, ACT_G[l], True)
                norm_sum(3 * l + 2)
                for m in range(WIDE + 1, KT):
                    step(tile_step(STEP_GATE[l], m), SLOT_GATE[l] + m, a_g, ACT_G[l], parts(l, m),
                         between={1: lambda: norm_spread(3 * l + 2)} if m == WIDE + 1 else {})
                if l == 0:
                    side_by_side(STEP_CONV, SLOT_CONV, act1, ACT_H[1],
                                 between={KT - 3: lambda: norm_sum(3), KT - 2: lambda: norm_spread(3)})

                    def conv_steps(m, js):
                        for j in js:
                            s, slot = STEP_CONV + j, SLOT_CONV + j
                            weights_ready(slot, 4 * m)
                            pe.wait_ge(pj_free[s % 2], 2 * m + s // 2)
                            end = products(ps_pj[s % 2], slot, act1, range(KT), 0, KT - 1)
                            end.then_inc(pj_done, 1)

                    conv_steps(0, [2, 3])
                    with pe.Fori(1, KT) as m:
                        conv_steps(m, range(4))


def slots(w):
    n = w.shape[1] // P
    return w.reshape(KT, P, n, P).transpose(2, 1, 0, 3).reshape(n, P, D)


def weight_stream(attn_w_in, attn_w_out, conv_w_in, conv_w_out, pe_w_gate, pe_w_proj):
    qkvz = slots(attn_w_in[0][:, :4 * D]).reshape(4, PAIRS, P, D).transpose(1, 0, 2, 3).reshape(4 * PAIRS, P, D)
    bchz = slots(conv_w_in[0]).reshape(4, KT, P, D)
    chbz = bchz[[1, 2, 0, 3]].transpose(1, 0, 2, 3).reshape(4 * KT, P, D)
    tails = []
    for i, w in enumerate((attn_w_out, conv_w_out)):
        tail = list(slots(w[0])) + list(slots(pe_w_gate[i]))
        for k in reversed(range(PLE_KT)):
            tail.insert(PLE_AFTER[k] + 1, pe_w_proj[i][k * P:(k + 1) * P])
        tails.append(np.stack(tail))
    return np.concatenate([qkvz, tails[0], chbz, tails[1]])


def kernel(**inputs):
    import concourse.bacc as bacc
    from concourse.bass_utils import run_bass_kernel_spmd

    a = {name: np.asarray(value) for name, value in inputs.items()}
    by_feature = lambda v: v.reshape(-1, KT, P).transpose(2, 0, 1)
    arrays = {
        "in_xT": a["x"][0].T.reshape(KT, P, SEQ),
        "in_pT": a["p"][:, 0].transpose(0, 2, 1).reshape(2, PLE_KT, P, SEQ).transpose(0, 2, 1, 3),
        "in_weights": weight_stream(a["attn_w_in"], a["attn_w_out"], a["conv_w_in"], a["conv_w_out"],
                                    a["pe_w_gate"], a["pe_w_proj"]),
        "in_f_weights": np.pad(a["attn_w_in"][0][:, 4 * D:].reshape(KT, P, HEADS).transpose(1, 0, 2),
                               ((0, 0), (0, 0), (0, F_PART - HEADS))),
        "in_b_f": a["attn_b_f"].reshape(HEADS, 1),
        "in_norm_pre": by_feature(a["norm_pre"]),
        "in_norm_post": by_feature(a["norm_post"]),
        "in_pe_norm": by_feature(a["pe_norm"]),
        "in_taps": by_feature(a["conv_kernel"][0]),
    }
    arrays = {name: np.ascontiguousarray(value) for name, value in arrays.items()}
    nc = bacc.Bacc("TRN2", target_bir_lowering=False, num_devices=1)
    args = [nc.dram_tensor(name, v.shape, mybir.dt.from_np(v.dtype), kind="ExternalInput").ap()
            for name, v in arrays.items()]
    out = nc.dram_tensor("out_0", (KT, P, SEQ), F32, kind="ExternalOutput").ap()
    trunk(nc, *args, out)
    result = run_bass_kernel_spmd(nc, [arrays], core_ids=[0])
    return result.results[0]["out_0"].reshape(D, SEQ).T.reshape(1, SEQ, D)
```
